# Optimizing a Trainium2 kernel written in Bass

```python
import jax, jax.numpy as jnp
from jax import lax
import numpy as np

D_MODEL = 1024
BATCH = 1
SEQ = 128
DEPTH = 1
DEC_BATCH = 1
DEC_SEQ = 512
PAST_LEN = 128

GRID_W = 64
NA_HEADS = 8
NA_HEAD_DIM = 64
NA_WIDTH = NA_HEADS * NA_HEAD_DIM
NA_KH = 8
NA_KW = 16
NA_QB = 16
NA_KB = NA_QB + NA_KW
NA_SCALE = NA_HEAD_DIM ** -0.5
Q_BLOCK = 128
M_HEADS = 4
M_DK = 128
M_DV = 128
M_WIDTH = M_HEADS * M_DV
M_CHUNK = 128
M_SCALE = M_DK ** -0.5
M_F_BIAS_LO = 3.0
M_F_BIAS_HI = 6.0
CONV_WIDTH = 512
CONV_K = 3
D_FF = ((8 * D_MODEL // 3 + 255) // 256) * 256
N_BRANCH = 3
N_MOD = 6
EPS = 1e-6
NEG = -1e30

SPLITS = ([NA_WIDTH] * 3
          + [M_HEADS * M_DK, M_HEADS * M_DK, M_WIDTH, M_WIDTH, 2 * M_HEADS, 2 * M_HEADS]
          + [CONV_WIDTH] * 3
          + [N_BRANCH * D_MODEL])
D_IN = sum(SPLITS)
SPLIT_IDX = np.cumsum(SPLITS)[:-1].tolist()

kernel_name = 'hybrid_na_mlstm_conv_diffusion_step'

def rmsnorm(x, g):
    xf = x.astype(jnp.float32)
    y = xf * lax.rsqrt(jnp.mean(xf * xf, axis=-1, keepdims=True) + EPS)
    return (y * g.astype(jnp.float32)).astype(x.dtype)

def split_heads(a, n):
    b, t, _ = a.shape
    return a.reshape(b, t, n, -1).transpose(0, 2, 1, 3)

def merge_heads(a):
    b, h, t, d = a.shape
    return a.transpose(0, 2, 1, 3).reshape(b, t, h * d)

def context_attention(q, k, v):
    B, H, S, dh = q.shape
    qb = jnp.moveaxis(q.reshape(B, H, S // Q_BLOCK, Q_BLOCK, dh), 2, 0)

    def block(qi):
        s = jnp.einsum('bhqd,bhkd->bhqk', qi, k).astype(jnp.float32)
        p = jax.nn.softmax(s, axis=-1).astype(v.dtype)
        return jnp.einsum('bhqk,bhkd->bhqd', p, v)

    o = lax.map(block, qb)
    return jnp.moveaxis(o, 0, 2).reshape(B, H, S, dh)

def neighborhood_attention(q, k, v, k_ctx, v_ctx, rpb):
    B, H, N, dh = q.shape
    rows = N // GRID_W
    kh = min(NA_KH, rows)
    nqb = GRID_W // NA_QB
    qcols = np.arange(GRID_W).reshape(nqb, NA_QB)
    kstart = np.clip(qcols[:, 0] - NA_KW // 2, 0, GRID_W - NA_KB)
    kcols = kstart[:, None] + np.arange(NA_KB)
    cs = np.clip(qcols - NA_KW // 2, 0, GRID_W - NA_KW)
    kk = kcols[:, None, :]
    col_mask = jnp.asarray(np.where((kk >= cs[:, :, None]) & (kk < cs[:, :, None] + NA_KW), 0.0, NEG),
                           dtype=jnp.float32)
    dc_idx = np.clip(kk - qcols[:, :, None] + NA_KW - 1, 0, 2 * NA_KW - 2)
    bias_c = rpb.astype(jnp.float32)[:, :, dc_idx]
    kg = k.reshape(B, H, rows, GRID_W, dh)[:, :, :, kcols]
    vg = v.reshape(B, H, rows, GRID_W, dh)[:, :, :, kcols]
    qg = jnp.moveaxis(q.reshape(B, H, rows, nqb, NA_QB, dh), 2, 0)
    n_loc = kh * NA_KB

    def row_block(args):
        r, qr = args
        rs = jnp.clip(r - kh // 2, 0, rows - kh)
        kr = lax.dynamic_slice_in_dim(kg, rs, kh, axis=2)
        vr = lax.dynamic_slice_in_dim(vg, rs, kh, axis=2)
        bias = jnp.take(bias_c, rs + jnp.arange(kh) - r + NA_KH - 1, axis=1).transpose(0, 2, 3, 1, 4)
        s_loc = (jnp.einsum('bhjqd,bhijkd->bhjqik', qr, kr).astype(jnp.float32)
                 + bias[None] + col_mask[None, None, :, :, None, :])
        s_ctx = jnp.einsum('bhjqd,bhpd->bhjqp', qr, k_ctx).astype(jnp.float32)
        p = jax.nn.softmax(jnp.concatenate([s_loc.reshape(B, H, nqb, NA_QB, n_loc), s_ctx], axis=-1),
                           axis=-1).astype(v.dtype)
        p_loc = p[..., :n_loc].reshape(B, H, nqb, NA_QB, kh, NA_KB)
        return (jnp.einsum('bhjqik,bhijkd->bhjqd', p_loc, vr)
                + jnp.einsum('bhjqp,bhpd->bhjqd', p[..., n_loc:], v_ctx))

    o = lax.map(row_block, (jnp.arange(rows), qg))
    return jnp.moveaxis(o, 0, 2).reshape(B, H, N, dh)

def mlstm_chunkwise(q, k, v, i_pre, log_f, C0, n0, m0):
    B, H, N, _ = q.shape
    dv = v.shape[-1]
    nc = N // M_CHUNK
    causal = jnp.asarray(np.tril(np.ones((M_CHUNK, M_CHUNK), dtype=bool)))

    def chunks(a):
        return jnp.moveaxis(a.reshape(a.shape[:2] + (nc, M_CHUNK) + a.shape[3:]), 2, 0)

    def step(carry, inp):
        C, n, m = carry
        qc, kc, vc, ic, fc = inp
        b = jnp.cumsum(fc, axis=-1)
        d = jnp.where(causal, b[..., :, None] - b[..., None, :] + ic[..., None, :], NEG)
        inter = b + m[..., None]
        mt = jnp.maximum(inter, jnp.max(d, axis=-1))
        w_int = jnp.exp(inter - mt)
        s = jnp.einsum('bhtd,bhsd->bhts', qc, kc) * jnp.exp(d - mt[..., None])
        num = w_int[..., None] * jnp.einsum('bhtd,bhde->bhte', qc, C) + jnp.einsum('bhts,bhse->bhte', s, vc)
        den = w_int * jnp.einsum('bhtd,bhd->bht', qc, n) + jnp.sum(s, axis=-1)
        h = num / jnp.maximum(jnp.abs(den), jnp.exp(-mt))[..., None]
        g = b[..., -1:] - b + ic
        m_new = jnp.maximum(b[..., -1] + m, jnp.max(g, axis=-1))
        wk = jnp.exp(g - m_new[..., None])
        decay = jnp.exp(b[..., -1] + m - m_new)
        C_new = decay[..., None, None] * C + jnp.einsum('bhs,bhsd,bhse->bhde', wk, kc, vc)
        n_new = decay[..., None] * n + jnp.einsum('bhs,bhsd->bhd', wk, kc)
        return (C_new, n_new, m_new), h

    xs = tuple(chunks(a) for a in (q, k, v, i_pre, log_f))
    (C, n, m), hs = lax.scan(step, (C0, n0, m0), xs)
    h = jnp.moveaxis(hs, 0, 2).reshape(B, H, N, dv)
    return h, C, n, m

def bidir_mlstm(q, k, v, i_pre, f_pre, C0, n0, m0):
    f32 = jnp.float32
    q, k, v, i_pre = q.astype(f32), k.astype(f32), v.astype(f32), i_pre.astype(f32)
    log_f = jax.nn.log_sigmoid(f_pre.astype(f32))
    C0, n0, m0 = C0.astype(f32), n0.astype(f32), m0.astype(f32)
    h_f, Cf, nf, mf = mlstm_chunkwise(q, k, v, i_pre[:, 0], log_f[:, 0], C0[:, 0], n0[:, 0], m0[:, 0])
    rev = lambda a: jnp.flip(a, axis=2)
    h_b, Cb, nb, mb = mlstm_chunkwise(rev(q), rev(k), rev(v), rev(i_pre[:, 1]), rev(log_f[:, 1]),
                                      C0[:, 1], n0[:, 1], m0[:, 1])
    h = h_f + rev(h_b)
    return h, jnp.stack([Cf, Cb], axis=1), jnp.stack([nf, nb], axis=1), jnp.stack([mf, mb], axis=1)

def short_conv(u, w):
    up = jnp.pad(u, ((0, 0), (1, 1), (0, 0)))
    return up[:, :-2] * w[0] + up[:, 1:-1] * w[1] + up[:, 2:] * w[2]

def trunk_layer(x, cond, P, l, ctx):
    B, N, _ = x.shape
    mod = (jax.nn.silu(cond) @ P['w_ada'][l] + P['b_ada'][l]).reshape(cond.shape[0], N_MOD, D_MODEL)
    shift1, scale1, gate1, shift2, scale2, gate2 = (mod[:, i, None, :] for i in range(N_MOD))

    h = rmsnorm(x, P['g_pre_mix'][l]) * (1 + scale1) + shift1
    (na_q, na_k, na_v, m_q, m_k, m_v, m_o, m_i, m_f, cv_b, cv_c, cv_x, gate_pre) = jnp.split(
        h @ P['w_in'][l], SPLIT_IDX, axis=-1)

    q = split_heads(na_q, NA_HEADS) * NA_SCALE
    k = split_heads(na_k, NA_HEADS)
    v = split_heads(na_v, NA_HEADS)
    if ctx is None:
        att = context_attention(q, k, v)
        C0 = jnp.zeros((B, 2, M_HEADS, M_DK, M_DV), jnp.float32)
        n0 = jnp.zeros((B, 2, M_HEADS, M_DK), jnp.float32)
        m0 = jnp.zeros((B, 2, M_HEADS), jnp.float32)
    else:
        k_ctx, v_ctx, C0, n0, m0 = ctx
        att = neighborhood_attention(q, k, v, k_ctx, v_ctx, P['na_rpb'][l])

    i_pre = (m_i.reshape(B, N, 2, M_HEADS) + P['m_b_i'][l]).transpose(0, 2, 3, 1)
    f_pre = (m_f.reshape(B, N, 2, M_HEADS) + P['m_b_f'][l]).transpose(0, 2, 3, 1)
    hm, C, n, m = bidir_mlstm(split_heads(m_q, M_HEADS) * M_SCALE, split_heads(m_k, M_HEADS),
                              split_heads(m_v, M_HEADS), i_pre, f_pre, C0, n0, m0)
    hm = hm * lax.rsqrt(jnp.mean(hm * hm, axis=-1, keepdims=True) + EPS)
    hm = merge_heads(hm).astype(x.dtype) * P['m_norm_g'][l] * jax.nn.sigmoid(m_o)

    hc = cv_b * short_conv(cv_c * cv_x, P['conv_w'][l])

    g = jax.nn.sigmoid(gate_pre + P['b_gate'][l]).reshape(B, N, N_BRANCH, D_MODEL)
    merged = (g[:, :, 0] * (merge_heads(att) @ P['w_br_na'][l])
              + g[:, :, 1] * (hm @ P['w_br_m'][l])
              + g[:, :, 2] * (hc @ P['w_br_cv'][l]))
    x = x + gate1 * rmsnorm(merged @ P['w_out'][l], P['g_post_mix'][l])

    h2 = rmsnorm(x, P['g_pre_ffn'][l]) * (1 + scale2) + shift2
    ff = (jax.nn.silu(h2 @ P['w_ffn_gate'][l]) * (h2 @ P['w_ffn_up'][l])) @ P['w_ffn_down'][l]
    x = x + gate2 * rmsnorm(ff, P['g_post_ffn'][l])
    new_ctx = (k, v, C, n, m) if ctx is None else None
    return x, new_ctx

def setup_inputs(seed: int = 0) -> dict:
    key = jax.random.key(seed)
    ks = jax.random.split(key, 32)
    nrm = lambda i, shape, s=1.0: jax.random.normal(ks[i], shape, jnp.float32) * s
    D = D_MODEL
    return {
        'x_prompt': nrm(0, (BATCH, SEQ, D)),
        'x_sample': nrm(1, (DEC_BATCH, DEC_SEQ, D)),
        'c': nrm(2, (DEC_BATCH, D)),
        'cache_k': nrm(3, (DEC_BATCH, DEPTH, NA_HEADS, PAST_LEN, NA_HEAD_DIM)),
        'cache_v': nrm(4, (DEC_BATCH, DEPTH, NA_HEADS, PAST_LEN, NA_HEAD_DIM)),
        'state_C': nrm(5, (DEC_BATCH, DEPTH, 2, M_HEADS, M_DK, M_DV), 0.5),
        'state_n': nrm(6, (DEC_BATCH, DEPTH, 2, M_HEADS, M_DK), 0.5),
        'state_m': jnp.abs(nrm(7, (DEC_BATCH, DEPTH, 2, M_HEADS), 0.5)),
        'c_ctx': nrm(8, (D,)),
        'w_ada': nrm(9, (DEPTH, D, N_MOD * D), D ** -0.5),
        'b_ada': nrm(10, (DEPTH, N_MOD * D), 0.02),
        'g_pre_mix': 1.0 + nrm(11, (DEPTH, D), 0.02),
        'g_post_mix': 1.0 + nrm(12, (DEPTH, D), 0.02),
        'g_pre_ffn': 1.0 + nrm(13, (DEPTH, D), 0.02),
        'g_post_ffn': 1.0 + nrm(14, (DEPTH, D), 0.02),
        'w_in': nrm(15, (DEPTH, D, D_IN), D ** -0.5),
        'b_gate': nrm(16, (DEPTH, N_BRANCH * D), 0.02),
        'm_b_i': nrm(17, (DEPTH, 2, M_HEADS), 0.1),
        'm_b_f': jnp.linspace(M_F_BIAS_LO, M_F_BIAS_HI, M_HEADS, dtype=jnp.float32) + nrm(18, (DEPTH, 2, M_HEADS), 0.1),
        'na_rpb': nrm(19, (DEPTH, NA_HEADS, 2 * NA_KH - 1, 2 * NA_KW - 1), 0.1),
        'm_norm_g': 1.0 + nrm(20, (DEPTH, M_WIDTH), 0.02),
        'conv_w': nrm(21, (DEPTH, CONV_K, CONV_WIDTH), CONV_K ** -0.5),
        'w_br_na': nrm(22, (DEPTH, NA_WIDTH, D), NA_WIDTH ** -0.5),
        'w_br_m': nrm(23, (DEPTH, M_WIDTH, D), M_WIDTH ** -0.5),
        'w_br_cv': nrm(24, (DEPTH, CONV_WIDTH, D), CONV_WIDTH ** -0.5),
        'w_out': nrm(25, (DEPTH, D, D), D ** -0.5),
        'w_ffn_gate': nrm(26, (DEPTH, D, D_FF), D ** -0.5),
        'w_ffn_up': nrm(27, (DEPTH, D, D_FF), D ** -0.5),
        'w_ffn_down': nrm(28, (DEPTH, D_FF, D), D_FF ** -0.5),
    }

def reference(x_prompt, x_sample, c, cache_k, cache_v, state_C, state_n, state_m, c_ctx,
              w_ada, b_ada, g_pre_mix, g_post_mix, g_pre_ffn, g_post_ffn, w_in, b_gate,
              m_b_i, m_b_f, na_rpb, m_norm_g, conv_w, w_br_na, w_br_m, w_br_cv, w_out,
              w_ffn_gate, w_ffn_up, w_ffn_down):
    P = dict(w_ada=w_ada, b_ada=b_ada, g_pre_mix=g_pre_mix, g_post_mix=g_post_mix,
             g_pre_ffn=g_pre_ffn, g_post_ffn=g_post_ffn, w_in=w_in, b_gate=b_gate,
             m_b_i=m_b_i, m_b_f=m_b_f, na_rpb=na_rpb, m_norm_g=m_norm_g, conv_w=conv_w,
             w_br_na=w_br_na, w_br_m=w_br_m, w_br_cv=w_br_cv, w_out=w_out,
             w_ffn_gate=w_ffn_gate, w_ffn_up=w_ffn_up, w_ffn_down=w_ffn_down)
    xp, xs = x_prompt, x_sample
    ks_, vs_, Cs_, ns_, ms_ = [], [], [], [], []
    for l in range(DEPTH):
        xp, (k_l, v_l, C_l, n_l, m_l) = trunk_layer(xp, c_ctx[None, :], P, l, None)
        ks_.append(k_l); vs_.append(v_l); Cs_.append(C_l); ns_.append(n_l); ms_.append(m_l)
        xs, _ = trunk_layer(xs, c, P, l, (cache_k[:, l], cache_v[:, l], state_C[:, l],
                                          state_n[:, l], state_m[:, l]))
    new_k = jnp.stack(ks_, axis=1)
    new_v = jnp.stack(vs_, axis=1)
    new_C = jnp.stack(Cs_, axis=1)
    new_n = jnp.stack(ns_, axis=1)
    new_m = jnp.stack(ms_, axis=1)
    return (xp, xs, new_k, new_v, new_C, new_n, new_m)


_drawn_inputs = setup_inputs


def setup_inputs(seed=0):
    import zlib

    import numpy as np

    out = dict(_drawn_inputs(seed))
    spreads = {}
    factors = {'state_C': 8.0,
     'state_n': 8.0,
     'state_m': 8.0,
     'g_post_mix': 4.893,
     'g_pre_ffn': 4.645,
     'g_post_ffn': 57.329,
     'b_gate': 8.0,
     'm_b_i': 3.091,
     'na_rpb': 64.0,
     'm_norm_g': 21.86,
     'cache_k': 2.989,
     'cache_v': 2.95}
    for name, (base, spread) in spreads.items():
        noise = np.random.default_rng([zlib.crc32(name.encode()), seed]).standard_normal(out[name].shape)
        drawn = base * np.exp(spread * noise) if base else spread * noise
        out[name] = __import__('jax').numpy.asarray(drawn.astype(out[name].dtype))
    for name, factor in factors.items():
        out[name] = (out[name] * factor).astype(out[name].dtype)
    return out
```

```python
import concourse.bass as bass
from concourse import mybir
from contextlib import ExitStack

F32 = mybir.dt.float32
F32R = mybir.dt.float32r
ALU = mybir.AluOpType
ACT = mybir.ActivationFunctionType
X = mybir.AxisListType.X

P = 128
D = 1024
KD = D // P
CTX, LAT = 128, 512
T = LAT + CTX
HT = T // 2
TT = T // P
EPS = 1e-6
HEADS, DH = 8, 64
GRID, ROWS = 64, LAT // 64
QB, KB, KW = 16, 32, 16
NQB = GRID // QB
KSTART = [min(max(j * QB - KW // 2, 0), GRID - KB) for j in range(NQB)]
SHIFT = [16 - (j * QB - KSTART[j]) for j in range(NQB)]
BTYPE = [0, 1, 1, 2]
NKEY = ROWS * KB + CTX
MH, DK = 4, 128
CH = LAT // P
RW = 36
FF = 2816
FK = FF // P
UW = 256
BIG = 1e30
NA_SCALE = DH ** -0.5
M_SCALE = DK ** -0.5

C_NAQ, C_NAK, C_NAV, C_MQ, C_MK, C_MV, C_MO, C_MIF = 0, 512, 1024, 1536, 2048, 2560, 3072, 3584
C_CB, C_CC, C_CX, C_GATE = 3600, 4112, 4624, 5136
R_BADA, R_GPM, R_GPF, R_BG, R_MG, R_CW, R_C = 0, 48, 56, 64, 88, 92, 104
NROWS = 120


def weight_units():
    u = []
    ada = lambda which, i: ("ada", (which, i), KD, UW)
    for i in range(4):
        u.append(ada(1, i))
    for i in range(4):
        u.append(ada(0, i))
    for p in range(2):
        u += [("q", p, KD, UW), ("k", p, KD, UW), ("v", p, KD, UW)]
    for kind in ("mq", "mk", "mv"):
        for p in range(2):
            u.append((kind, p, KD, UW))
    u.append(("mif", 0, KD, P))
    for p in range(2):
        u += [("cc", p, KD, UW), ("cx", p, KD, UW), ("cb", p, KD, UW)]
    late = {2: [[(4, i)] for i in range(4)], 0: [[(3, i)] for i in range(4)],
            1: [[(2, i), (5, i)] for i in range(4)]}
    for b in (2, 0, 1):
        if b == 0:
            u += [("mo", 0, KD, UW), ("mo", 1, KD, UW)]
        for i in range(4):
            u.append(("gate", (b, i), KD, UW))
            extra = [ada(*x) for x in late[b][i]]
            u += extra[:1]
            u.append(("br", (b, i), 4, UW))
            u += extra[1:]
    for c in range(2):
        for h in range(2):
            u.append(("out", (c, h), 4, 512))
    for i in range(FK // 2):
        u += [("fg", i, KD, UW), ("fu", i, KD, UW)]
    for c in range(2):
        for i in range(6):
            u.append(("down", (c, i), 4 if i < 5 else 2, 512))
    return u


UNITS = weight_units()
UNIT_OF = {(k, w): n for n, (k, w, _, _) in enumerate(UNITS)}
NA_UNITS = ([("lat", hp, j) for hp in (0, 1) for j in range(NQB)] + [("ctx", 0, 0)]
            + [("lat", hp, j) for hp in (2, 3) for j in range(NQB)] + [("ctx", 1, 0)])
ML_UNITS = []
for dr in range(2):
    for hp in range(2):
        ML_UNITS.append((CH, dr, hp, True, True))
for st in range(CH):
    for dr in range(2):
        for hp in range(2):
            ML_UNITS.append((st if dr == 0 else CH - 1 - st, dr, hp, st == 0, st == CH - 1))


def drain_engine(kind, what):
    if kind in ("out", "down"):
        return "V" if what[0] == 1 else "A"
    return "V" if kind in ("cx", "cb", "br", "mif", "vt", "mvt", "ada_col", "fu", "kout") else "A"


FIRST_DOWN = ([0, 1], [2, 3, 4])


def make_plan():
    plan, groups = [], []

    def group(kind, unit, *what, bank=None):
        g = len(groups)
        groups.append(dict(kind=kind, unit=unit, what=what, eng=drain_engine(kind, what),
                           bank=g % 4 if bank is None else bank))
        plan.append(("group", g))
        return g

    def tiles(n):
        kind = UNITS[n][0]
        for f in range(2 if kind != "mif" else 1):
            for h in range(2):
                yield lambda f=f, h=h: group(kind, n, f, h)

    side = []

    def unit(n):
        plan.append(("unit", n))
        if UNITS[n][:2] == ("cc", 0):
            plan.append(("mstat",))
        for emit in tiles(n):
            if side:
                plan.append(side.pop(0))
            emit()
            x = groups[-1]
            kind, turn = x["kind"], {"v": ("vt", 3), "mv": ("mvt", 2)}.get(x["kind"])
            if turn and x["what"] in ((1, 0), (1, 1)):
                for c in range(turn[1]):
                    group(turn[0], n, x["what"][1], c)

    plan.append(("prologue",))
    for n in range(8):
        plan.append(("unit", n))
        group("ada_row", n)
        if n:
            group("ada_col", n - 1)
        if n > 4:
            plan.append(("h", n - 5))
    group("ada_col", 7)
    plan.append(("h", 3))
    n = 8
    pending = []
    while UNITS[n][0] != "out":
        kind, which = UNITS[n][0], UNITS[n][1]
        if kind == "ada":
            plan.append(("unit", n))
            group("ada_row", n)
            pending.append(n)
        else:
            if kind == "mif":
                for s in side:
                    plan.append(s)
                side = []
                group("kout", n)
                plan.append(("na_end",))
            unit(n)
            while pending:
                group("ada_col", pending.pop(0))
        if kind == "v":
            if which == 0:
                N = len(NA_UNITS)
                for s in range(N + 2):
                    side += [("na", 0, s), ("na", 1, s)]
        if kind == "cc" and which == 0:
            plan.append(("mcols",))
            for s in range(len(ML_UNITS)):
                side += [("ml", 0, s), ("ml", 1, s)]
        if kind == "mo" and which == 0:
            assert not side
            for c in range(TT):
                side.append(("hm", 0, c))
        if kind == "mo" and which == 1:
            for c in range(TT):
                side.append(("hm", 1, c))
        n += 1
    while pending:
        group("ada_col", pending.pop(0))
    plan.append(("out_start",))
    for c in range(2):
        for h in range(2):
            plan.append(("unit", UNIT_OF[("out", (c, h))]))
            for t in range(TT + 3 if c and h else TT):
                if h == 0:
                    plan.append(("part", "out", c, t))
                else:
                    if t < TT:
                        group("out", UNIT_OF[("out", (c, h))], c, t, bank=(5 * c + t) % 8)
                    if c == 1:
                        for d, stage in enumerate(("resid", "square2", "turn2", "split2")):
                            if 0 <= t - d < TT:
                                plan.append((stage, t - d))
    for i in range(FK // 2):
        for k in ("fg", "fu"):
            m = UNIT_OF[(k, i)]
            plan.append(("unit", m))
            for h in range(2):
                for f in range(2):
                    group(k, m, f, h, bank=(4 if k == "fu" else 0) + 2 * h + f)
                if (k, i) == ("fu", FK // 2 - 1):
                    for piece in FIRST_DOWN[h]:
                        plan.append(("down_start", piece))
    for c in range(2):
        for i in range(6):
            m = UNIT_OF[("down", (c, i))]
            plan.append(("unit", m))
            for t in range(TT):
                if i == 5:
                    group("down", m, c, t, bank=(5 * c + t) % 8)
                    if c == 1:
                        plan.append(("final", t))
                else:
                    plan.append(("part", "down", c, t, i))
    return plan, groups


PLAN, GROUPS = make_plan()


def drains(eng, g):
    return sum(1 for x in GROUPS[:g + 1] if x["eng"] == eng)


def group_of(kind, which, f=1, h=1):
    u = UNIT_OF[(kind, which)]
    return max(g for g, x in enumerate(GROUPS) if x["unit"] == u and x["what"][:2] == (f, h))


def last_user(bank, g):
    prev = [i for i in range(g) if GROUPS[i]["bank"] == bank]
    return prev[-1] if prev else None


def drained_before(eng, g):
    return drains(eng, g)


def tail_count(n):
    mine = [g for g, x in enumerate(GROUPS) if x["unit"] == n and x["kind"] not in ("ada_col", "vt", "mvt", "kout")]
    if mine:
        return "gemm", max(mine) + 1
    count = 0
    for step in PLAN:
        if step[0] == "unit":
            now = step[1]
        if step[0] == "part":
            count += 1
            if now == n:
                value = count
    return "part", value


def lo_engine(n):
    return "V" if UNITS[n][0] in ("ada", "gate", "br", "mif") or n < UNIT_OF[("mif", 0)] else "P"


def lo_ready(n):
    e = lo_engine(n)
    return e, sum(1 for i in range(n + 1) if lo_engine(i) == e)


ADA = [n for n, u in enumerate(UNITS) if u[0] == "ada"]


def ada_slot(n):
    return ADA.index(n) % 2


RELEASE = [tail_count(n) for n in range(len(UNITS))]
LAST = {}
for _g, _x in enumerate(GROUPS):
    LAST[(_x["kind"], UNITS[_x["unit"]][1] if _x["kind"] not in ("kout",) else 0, _x["what"])] = _g


def gid(kind, which, *what):
    return LAST[(kind, which, what)]


def program(nc, a, out):
    ctx = ExitStack()
    with ctx:
        base = (nc.sbuf_base + 31) // 32 * 32 if not callable(nc.sbuf_base) else 16512
        arena = ctx.enter_context(nc.sbuf_tensor("arena", [P, 212832 // 4], F32))
        top = base + 212832

        def at(name, shape, offset, dt=F32):
            size = 4
            for n in shape[1:]:
                size *= n
            assert offset + size <= 212832, name
            return nc.alloc_sbuf_tensor_at(name, shape, dt, offset=base + offset)

        def chain(start, *items):
            got = []
            for name, shape, dt in items:
                got.append(at(name, shape, start, dt))
                size = 4
                for n in shape[1:]:
                    size *= n
                start += (size + 31) // 32 * 32
            return got, start

        (raw, w_hi, w_lo, h_hi, h_lo), R0 = chain(
            0, ("raw", [P, 2, 2048], F32), ("w_hi", [P, 2, 2048], F32R), ("w_lo", [P, 2, 2048], F32R),
            ("h_hi", [P, KD, T], F32R), ("h_lo", [P, KD, T], F32R))
        (cst, cols, mod, half_bg, cond, sil, small, adarow, gbias, neghalf), R1 = chain(
            R0, ("cst", [P, 736], F32), ("cols", [P, NROWS], F32), ("mod", [P, 4, KD, 2], F32),
            ("half_bg", [P, 24], F32), ("cond", [P, KD, 4], F32R), ("sil", [P, 16], F32),
            ("small", [P, 64], F32), ("adarow", [4, 2, UW], F32), ("gbias", [RW, 3], F32),
            ("neghalf", [P, 8], F32))
        ident = cst[:, 0:128]
        mask_m = cst[:, 128:384].rearrange("p (d t) -> p d t", d=2)
        mask_na = cst[:, 384:480].rearrange("p (y k) -> p y k", y=3)
        sel = cst[0:4, 480:736].rearrange("p (c m) -> p c m", c=2)
        (naq, nak, vtok, kct, vg, bm, braw, sx, pt), _e = chain(
            R1, ("naq", [P, 4, T], F32), ("nak", [P, 4, T], F32), ("vtok", [P, 10, 512], F32),
            ("kct", [P, 4, CTX], F32), ("vg", [P, 9, P], F32), ("bm", [P, 3, 2, NKEY], F32),
            ("braw", [P, 2, 512], F32), ("sx", [P, 2, 2, NKEY], F32), ("pt", [P, 2, 2, NKEY], F32))
        MQ = 212832 - 10240 * 3 - 10336
        assert _e <= MQ, _e
        (mq, mk, mv, att), _ = chain(
            MQ, ("mq", [P, MH, T], F32), ("mk", [P, MH, T], F32), ("mv", [P, TT, MH, 129], F32),
            ("att", [P, 4, T], F32))
        xt = at("xt", [P, TT, D], R1)
        xnt = at("xnt", [P, KD, T], R1 + 20480)
        rows = at("rows", [NROWS, P], R1 + 61440)
        kcr = at("kcr", [P, 512], R1 + 62464)
        junk = at("junk", [P, D], MQ)
        (bo_hi, bo_lo, cl, cout, hsum, mnat, mcols, dec, e_sb, st_sb, kw_sb, tmp_sb, num_sb, merged, gt), _e = chain(
            R1, ("bo_hi", [P, 4, T], F32R), ("bo_lo", [P, 4, T], F32R), ("cl", [P, 8, 129], F32),
            ("cout", [P, 2, 2, 129], F32), ("hsum", [P, TT, 512], F32), ("mnat", [RW, T], F32),
            ("mcols", [P, TT, 4, 8], F32), ("dec", [P, 8, CH], F32), ("e_sb", [P, 2, 2, P], F32),
            ("st_sb", [P, 2, 2, P], F32), ("kw_sb", [P, 2, 2, P], F32), ("tmp_sb", [P, 2, 129], F32),
            ("num_sb", [P, 2, 129], F32), ("merged", [P, KD, T], F32), ("gt", [P, 2, T], F32))
        assert _e <= MQ, (_e, MQ)
        MG = _e - 5120 - 20480
        cu = at("cu", [P, 2, T], MG)
        t1 = at("t1", [P, 2, T], MG + 5120)
        ib = at("ib", [RW, T], R1 + 20480 * 2 + 2048)
        lf = at("lf", [RW, T], R1 + 20480 * 2 + 2048 + 2560)
        st = [at(f"stat{i}", [RW, T], R1 + 2560 * i) for i in range(7)]
        mo = at("mo", [P, MH, T], MQ)
        hmt = at("hmt", [P, MH, T], MQ + 10240)
        g1 = at("g1", [P, 2, D], MQ + 20480)
        bb1 = at("bb1", [P, 2, D], MQ + 20480 + 10336)
        g2 = at("g2", [P, 2, D], R1 + 20480)
        bb2 = at("bb2", [P, 2, D], R1 + 20480 + 8192)
        x1 = at("x1", [P, TT, D], R1)
        (xb, xn, junk2), _e = chain(
            R1 + 20480 + 8192, ("xb", [P, 2, D], F32), ("xn", [P, 2, D], F32), ("junk2", [P, D], F32))
        h32 = at("h32", [P, 2, KD, P], _e)
        (ff, sg, y2, yb, yb_junk), _e = chain(
            R1 + 20480 + 8192, ("ff", [P, FK, T], F32), ("sg", [P, 4, HT], F32),
            ("y2", [P, TT, 512], F32), ("yb", [P, 512], F32), ("yb_junk", [P, 512], F32))
        assert _e <= 212832
        ps = ctx.enter_context(nc.psum_tensor("ps", [P, 8, 512], F32))
        A = [ps[:, 4 + i, :] for i in range(4)]

        def sem(name):
            return ctx.enter_context(nc.semaphore(name))

        const_in, rows_in, kc_in, gb_in = sem("const_in"), sem("rows_in"), sem("kc_in"), sem("gb_in")
        x_in = [sem(f"x_in{t}") for t in range(TT)]
        raw_in = [sem("raw_in0"), sem("raw_in1")]
        mif_zero = sem("mif_zero")
        vc_in, br_in, state_in = sem("vc_in"), sem("br_in"), sem("state_in")
        bc1_in, bc2_in = sem("bc1_in"), sem("bc2_in")
        xb_in = [sem("xb_in0"), sem("xb_in1")]
        hi_done, lo_by = sem("hi_done"), dict(V=sem("lo_by_vector"), P=sem("lo_by_pool"))
        gemm_done, part_done = sem("gemm_done"), sem("part_done")
        act_drain, dve_drain = sem("act_drain"), sem("dve_drain")
        act_order, dve_order, pool_order = sem("act_order"), sem("dve_order"), sem("pool_order")
        cols_tr, cols_rd, cond_hi, cond_rd = sem("cols_tr"), sem("cols_rd"), sem("cond_hi"), sem("cond_rd")
        kc_tr, kc_rd = sem("kc_tr"), sem("kc_rd")
        x_sq, x_rstd, x_nrm = sem("x_sq"), sem("x_rstd"), sem("x_nrm")
        xl_tr, xc_tr, xt_dve, xt_act, xc_dve = (sem("xl_tr"), sem("xc_tr"), sem("xt_dve"), sem("xt_act"),
                                                sem("xc_dve"))
        h_aff, h_hid, h_lod = sem("h_aff"), sem("h_hid"), sem("h_lod")
        bias_rd, bias_zero, mv_ones, nh_rd = sem("bias_rd"), sem("bias_zero"), sem("mv_ones"), sem("nh_rd")
        na_sc, na_add, na_max, na_exp, na_prob, na_tr, na_pt, na_pv, na_out = [
            sem(n) for n in ("na_sc", "na_add", "na_max", "na_exp", "na_prob", "na_tr", "na_pt", "na_pv", "na_out")]
        f_neg, f_exp, f_ln, s_exp_in, s_exp, nat_rd, ms_tr, ms_rd, m_fin = [
            sem(n) for n in ("f_neg", "f_exp", "f_ln", "s_exp_in", "s_exp", "nat_rd", "ms_tr", "ms_rd", "m_fin")]
        ml_a, ml_dm, ml_e, ml_kw, ml_st, ml_b, ml_tmp, ml_c, ml_h = [
            sem(n) for n in ("ml_a", "ml_dm", "ml_e", "ml_kw", "ml_st", "ml_b", "ml_tmp", "ml_c", "ml_h")]
        conv_rd, bo_hid, bo_lod, merged_add = sem("conv_rd"), sem("bo_hid"), sem("bo_lod"), sem("merged_add")
        mo_rd, hm_sq, hm_rstd, hm_nrm, hm_tr, hm_out = [
            sem(n) for n in ("mo_rd", "hm_sq", "hm_rstd", "hm_nrm", "hm_tr", "hm_out")]
        mg_hid, mg_lod, y_sq, y_rstd, x1_rd, x1_sq, x1_rstd, xn_rd, n2_tr, n2_ev, n2_hid, n2_lod = [
            sem(n) for n in ("mg_hid", "mg_lod", "y_sq", "y_rstd", "x1_rd", "x1_sq", "x1_rstd", "xn_rd",
                             "n2_tr", "n2_ev", "n2_hid", "n2_lod")]
        ffs_hi, ffs_lo, z_sq, z_rstd, fin_rd = [
            sem(n) for n in ("ffs_hi", "ffs_lo", "z_sq", "z_rstd", "fin_rd")]
        stored, c_out = sem("stored"), [sem("c_out0"), sem("c_out1")]
        block = ctx.enter_context(nc.Block())

        def half(h):
            return slice(h * HT, (h + 1) * HT)

        def tok(t):
            return slice(t * P, (t + 1) * P)

        def wait_release(eng, n):
            kind, value = RELEASE[n]
            eng.wait_ge(gemm_done if kind == "gemm" else part_done, value)

        def wait_lo(eng, n):
            e, value = lo_ready(n)
            eng.wait_ge(lo_by[e], value)

        def split_low(ve, eng, n):
            eng.wait_ge(hi_done, n + 1)
            if UNITS[n][0] == "mif":
                v = lambda buf: slot(buf, n).rearrange("p k (g c) -> p k g c", g=4)[:, :, :, 0:4]
                r = raw[:, n % 2, 0:128].rearrange("p (k g c) -> p k g c", k=KD, g=4)
                for k in range(KD):
                    ins = ve.tensor_tensor(v(w_lo)[:, k], r[:, k], v(w_hi).bitcast(F32)[:, k], ALU.subtract)
            else:
                m = UNITS[n][2] * UNITS[n][3]
                ins = ve.tensor_tensor(w_lo[:, n % 2, 0:m], raw[:, n % 2, 0:m],
                                       w_hi[:, n % 2, 0:m].bitcast(F32), ALU.subtract)
            ins.then_inc(lo_by[lo_engine(n)], 1)

        def slot(buf, n):
            kc, w = UNITS[n][2], UNITS[n][3]
            return buf[:, n % 2, 0:kc * w].rearrange("p (k w) -> p k w", k=kc)

        def source(n):
            kind, which, kc, w = UNITS[n]
            if kind == "ada":
                m, k0, c0 = "w_ada", 0, which[0] * D + which[1] * UW
            elif kind == "br":
                m, k0, c0 = ("w_br_na", "w_br_m", "w_br_cv")[which[0]], 0, which[1] * UW
            elif kind == "out":
                m, k0, c0 = "w_out", 4 * which[1], which[0] * 512
            elif kind == "fg":
                m, k0, c0 = "w_ffn_gate", 0, which * UW
            elif kind == "fu":
                m, k0, c0 = "w_ffn_up", 0, which * UW
            elif kind == "down":
                m, k0, c0 = "w_ffn_down", 4 * which[1], which[0] * 512
            elif kind == "gate":
                m, k0, c0 = "w_in", 0, C_GATE + which[0] * D + which[1] * UW
            elif kind == "mif":
                m, k0, c0, w = "w_in", 0, C_MIF, 16
            else:
                m, k0 = "w_in", 0
                c0 = dict(q=C_NAQ, k=C_NAK, v=C_NAV, mq=C_MQ, mk=C_MK, mv=C_MV, mo=C_MO, cc=C_CC, cx=C_CX,
                          cb=C_CB)[kind] + which * UW
            return a[m][0, k0 * P:(k0 + kc) * P, c0:c0 + w].rearrange("(k p) w -> p k w", p=P)

        def row_to_all(name, c0):
            return bass.AP(a[name].tensor, c0, [[0, P], [1, D]])

        @block.sync
        def _(sp):
            sp.dma_start(cst[:, :], a["consts"]).then_inc(const_in, 16)
            sp.dma_start(rows[:, :], a["rows"]).then_inc(rows_in, 16)
            for t in range(TT):
                src = a["x_sample"][0, tok(t), :] if t < CH else a["x_prompt"][0]
                sp.dma_start(xt[:, t, :], src).then_inc(x_in[t], 16)
            sp.dma_start(kcr[:, :].rearrange("p (h d) -> p h d", h=HEADS),
                         a["cache_k"][0, 0].rearrange("h p d -> p h d")).then_inc(kc_in, 16)

            def load(n):
                if n >= 2:
                    wait_lo(sp, n - 2)
                dst = raw[:, n % 2, 0:128].rearrange("p (k w) -> p k w", k=KD) if UNITS[n][0] == "mif" \
                    else slot(raw, n)
                sp.dma_start(dst, source(n)).then_inc(raw_in[n % 2], 16)

            def load_x(t):
                if t >= 2:
                    sp.wait_ge(x1_rd, t - 1)
                src = a["x_sample"][0, tok(t), :] if t < CH else a["x_prompt"][0]
                sp.dma_start(xb[:, t % 2, :], src).then_inc(xb_in[t % 2], 16)

            load(0)
            load(1)
            for step in PLAN:
                if step[0] == "unit":
                    if step[1] + 2 < len(UNITS):
                        load(step[1] + 2)
                elif step[0] == "na_end":
                    g = gid("kout", 0)
                    sp.wait_ge(dve_drain, drains("V", g))
                    sp.dma_start(out["k"][0, 0].rearrange("h s d -> s h d"),
                                 sx[:, 0, :, :].rearrange("p a k -> p (a k)")[:, 0:512].rearrange(
                                     "p (h d) -> p h d", h=HEADS)).then_inc(stored, 16)
                    sp.dma_start(out["v"][0, 0].rearrange("h s d -> s h d"),
                                 vtok[:, 8, :].rearrange("p (h d) -> p h d", h=HEADS)).then_inc(stored, 16)
                elif step[0] == "ml" and step[1] == 1 and ML_UNITS[step[2]][0] == CH:
                    n = step[2]
                    _, dr, hp, _, _ = ML_UNITS[n]
                    sp.wait_ge(ml_c, n + 1)
                    sp.dma_start(out["C"][0, 0, dr, 2 * hp:2 * hp + 2].rearrange("h d e -> d h e"),
                                 cout[:, n % 2, :, 0:128]).then_inc(c_out[n % 2], 16)
                    sp.dma_start(out["n"][0, 0, dr, 2 * hp:2 * hp + 2].rearrange("h d -> d h"),
                                 cout[:, n % 2, :, 128], allow_slow_non_contiguous=True).then_inc(c_out[n % 2], 16)
                elif step[0] == "out_start":
                    sp.wait_ge(mg_lod, 1)
                    load_x(0)
                    load_x(1)
                elif step[0] == "resid" and step[1] + 2 < TT:
                    load_x(step[1] + 2)
                elif step[0] == "final":
                    t = step[1]
                    sp.wait_ge(fin_rd, t + 1)
                    dst = out["ys"][0, tok(t), :] if t < CH else out["yp"][0]
                    sp.dma_start(dst, x1[:, t, :]).then_inc(stored, 16)
            sp.wait_ge(m_fin, 1)
            sp.dma_start(out["m"][0, 0, 0, :].rearrange("(h o) -> h o", o=1), small[0:4, 40:41]).then_inc(stored, 16)
            sp.dma_start(out["m"][0, 0, 1, :].rearrange("(h o) -> h o", o=1), small[32:36, 40:41]).then_inc(stored, 16)
            for s in c_out:
                sp.wait_ge(s, 64)
            sp.wait_ge(stored, 16 * (2 + TT + 2))

        @block.gpsimd
        def _(pool):
            seen = [0]

            def link(ins):
                seen[0] += 1
                ins.then_inc(pool_order, 1)
                pool.wait_ge(pool_order, seen[0])

            def rstd(dst, src, width, n):
                link(nc.gpsimd.tensor_scalar(dst, src, 1.0 / n, EPS, ALU.mult, ALU.add))
                return nc.gpsimd.tensor_tensor(dst, dst, neghalf[:, 0:width], ALU.pow)

            link(nc.gpsimd.memset(neghalf[:, :], -0.5))
            nc.gpsimd.memset(bm[:, :, :, 256:NKEY], 0.0).then_inc(bias_zero, 1)
            nc.gpsimd.memset(mv[:, :, :, 128:129], 1.0).then_inc(mv_ones, 1)
            pool.dma_start(gbias[:, :], a["gbias"]).then_inc(gb_in, 16)
            pool.wait_ge(x_sq, TT)
            rstd(small[:, 8:8 + TT], small[:, 0:TT], TT, D).then_inc(x_rstd, 1)

            def load_bias(hp):
                for i in range(2):
                    for r in range(ROWS):
                        src = bass.AP(a["rpb"].tensor, (2 * hp + i) * 1024 + (7 - r) * 64, [[1, QB], [1, 512]])
                        pool.dma_start(braw[16 * r:16 * r + 16, i, :], src).then_inc(br_in, 16)

            def bias(hp):
                pool.wait_ge(br_in, 16 * 2 * ROWS * (hp + 1))
                first = [0, 4, 9, 13][hp]
                for y, free in ((0, 1), (1, 3), (2, 4)):
                    if hp:
                        pool.wait_ge(na_add, [0, 4, 9, 13][hp - 1] + free)
                    sh = (16, 8, 0)[y]
                    for i in range(2):
                        ins = nc.gpsimd.tensor_tensor(
                            bm[:, y, i, 0:256].rearrange("p (r k) -> p r k", r=ROWS),
                            braw[:, i, :].rearrange("p (r k) -> p r k", r=ROWS)[:, :, sh:sh + KB],
                            mask_na[:, y, :].unsqueeze(1).to_broadcast([P, ROWS, KB]), ALU.add)
                    ins.then_inc(bias_rd, 1)

            pool.wait_ge(const_in, 16)
            pool.wait_ge(kc_rd, 1)
            load_bias(0)
            pool.wait_ge(h_lod, KD)
            pool.dma_start(vtok[:, 9, :].rearrange("p (h d) -> p h d", h=HEADS),
                           a["cache_v"][0, 0].rearrange("h p d -> p h d")).then_inc(vc_in, 16)
            bias(0)
            pool.wait_ge(bias_rd, 3)
            load_bias(1)
            for step in PLAN:
                if step[0] == "unit" and step[1] + 1 < len(UNITS) and lo_engine(step[1] + 1) == "P":
                    split_low(nc.gpsimd, pool, step[1] + 1)
                if step[0] == "na" and step[1] == 1 and step[2] in (1, 5, 10):
                    hp = {1: 1, 5: 2, 10: 3}[step[2]]
                    bias(hp)
                    if hp < 3:
                        pool.wait_ge(bias_rd, 3 * (hp + 1))
                        load_bias(hp + 1)
                elif step == ("unit", UNIT_OF[("mif", 0)] - 1):
                    n = UNIT_OF[("mif", 0)]
                    wait_release(pool, n - 2)
                    nc.gpsimd.memset(w_hi[:, n % 2, 0:KD * P].bitcast(F32), 0.0).then_inc(mif_zero, 1)
                    nc.gpsimd.memset(w_lo[:, n % 2, 0:KD * P].bitcast(F32), 0.0).then_inc(mif_zero, 1)
                elif step[0] == "mstat":
                    pool.wait_ge(stored, 32)
                    pool.wait_ge(na_out, len(NA_UNITS))
                    pool.dma_start(cl[:, :, 0:128],
                                   a["state_C"][0, 0].rearrange("a h d e -> d (a h) e")).then_inc(state_in, 16)
                    pool.dma_start(cl[:, :, 128], a["state_n"][0, 0].rearrange("a h d -> d (a h)"),
                                   allow_slow_non_contiguous=True).then_inc(state_in, 16)
                elif step[0] == "unit" and UNITS[step[1]][:2] == ("gate", (1, 0)):
                    pool.wait_ge(bo_lod, 8)
                    pool.dma_start(bb1[:, 0, :], row_to_all("b_ada", 2 * D)).then_inc(bc1_in, 16)
                    pool.dma_start(bb1[:, 1, :], row_to_all("g_post_mix", 0)).then_inc(bc1_in, 16)
                    pool.wait_ge(hm_tr, TT)
                    pool.dma_start(bb2[:, 0, :], row_to_all("b_ada", 5 * D)).then_inc(bc2_in, 16)
                    pool.dma_start(bb2[:, 1, :], row_to_all("g_post_ffn", 0)).then_inc(bc2_in, 16)
                elif step[0] == "group" and GROUPS[step[1]]["kind"] == "mo":
                    x = GROUPS[step[1]]
                    f, h = x["what"]
                    pool.wait_ge(act_drain, drains("A", step[1]))
                    v = mo[:, 2 * UNITS[x["unit"]][1] + f, half(h)]
                    nc.gpsimd.tensor_scalar(v, v, 0.5, 0.5, ALU.mult, ALU.add).then_inc(mo_rd, 1)
                elif step[0] == "hm" and step[1] == 0:
                    c = step[2]
                    pool.wait_ge(hm_sq, c + 1)
                    v = small[:, 16 + 4 * c:20 + 4 * c] if c < 4 else small[:, 32:36]
                    rstd(v, v, 4, 128).then_inc(hm_rstd, 1)
                elif step[0] == "resid":
                    t = step[1]
                    pool.wait_ge(y_sq, t + 1)
                    v = small[:, t:t + 1]
                    link(nc.gpsimd.tensor_tensor(v, small[:, 44 + t:45 + t], small[:, 49 + t:50 + t], ALU.add))
                    rstd(v, v, 1, D).then_inc(y_rstd, 1)
                elif step[0] == "square2":
                    t = step[1]
                    pool.wait_ge(x1_sq, t + 1)
                    v = small[:, 8 + t:9 + t]
                    rstd(v, v, 1, D).then_inc(x1_rstd, 1)
                elif step[0] == "final":
                    t = step[1]
                    pool.wait_ge(z_sq, t + 1)
                    v = small[:, 16 + t:17 + t]
                    link(nc.gpsimd.tensor_tensor(v, small[:, 24 + t:25 + t], small[:, 32 + t:33 + t], ALU.add))
                    rstd(v, v, 1, D).then_inc(z_rstd, 1)

        @block.scalar
        def _(act):
            seen = [0]

            def link(ins):
                seen[0] += 1
                ins.then_inc(act_order, 1)
                act.wait_ge(act_order, seen[0])

            def split_hi(n):
                act.wait_ge(raw_in[n % 2], 16 * (n // 2 + 1))
                if n >= 2:
                    wait_release(act, n - 2)
                if UNITS[n][0] == "mif":
                    act.wait_ge(mif_zero, 2)
                    w = slot(w_hi, n).rearrange("p k (g c) -> p k g c", g=4)[:, :, :, 0:4]
                    r = raw[:, n % 2, 0:128].rearrange("p (k g c) -> p k g c", k=KD, g=4)
                    for k in range(KD):
                        ins = nc.scalar.activation(w[:, k], r[:, k], ACT.Copy)
                else:
                    m = UNITS[n][2] * UNITS[n][3]
                    ins = nc.scalar.activation(w_hi[:, n % 2, 0:m], raw[:, n % 2, 0:m], ACT.Copy)
                ins.then_inc(hi_done, 1)

            def branch_hi(src, last_group, ready, k0):
                act.wait_ge(gemm_done, last_group + 1)
                act.wait_ge(*ready)
                for k in range(4):
                    nc.scalar.activation(bo_hi[:, k, :], src[:, k, :], ACT.Copy).then_inc(bo_hid, 1)

            def first_ff_hi(t):
                act.wait_ge(gemm_done, gid("fu", FK // 2 - 1, 1, 0 if t in FIRST_DOWN[0] else 1) + 1)
                act.wait_ge(dve_drain, drains("V", gid("fu", 1, 1, 1)))
                nc.scalar.activation(h_hi[:, 0:4, tok(t)], ff[:, 0:4, tok(t)], ACT.Copy).then_inc(ffs_hi, 1)

            def ff_hi(o):
                c, i = divmod(o, 6)
                kc = 4 if i < 5 else 2
                if o < 2:
                    act.wait_ge(gemm_done, gid("fu", FK // 2 - 1, 1, 1) + 1)
                else:
                    wait_release(act, UNIT_OF[("down", divmod(o - 2, 6))])
                act.wait_ge(dve_drain, drains("V", gid("fu", FK // 2 - 1, 1, 1)))
                o2 = 4 * (o % 2)
                nc.scalar.activation(h_hi[:, o2:o2 + kc, :], ff[:, 4 * i:4 * i + kc, :], ACT.Copy).then_inc(ffs_hi, 1)

            def drain(g):
                x = GROUPS[g]
                kind, n = x["kind"], x["unit"]
                if x["eng"] != "A" and kind not in ("out", "down", "cb"):
                    return
                which = UNITS[n][1]
                bank = ps[:, x["bank"], 0:HT]
                if kind == "q":
                    f, h = x["what"]
                    act.wait_ge(gemm_done, g + 1)
                    r0, r1 = (0, 5) if h == 0 else (5, ROWS)
                    v = naq[:, 2 * which + f, 0:LAT].rearrange(
                        "p (j r c) -> p j r c", j=NQB, r=ROWS)[:, :, r0:r1, ::-1]
                    src = bank[:, 0:(r1 - r0) * GRID].rearrange("p (r j c) -> p j r c", j=NQB, c=QB)
                    ins = nc.scalar.activation(v, src, ACT.Copy, scale=NA_SCALE)
                    if h == 1:
                        ins = nc.scalar.activation(naq[:, 2 * which + f, LAT:T], bank[:, HT - P:HT], ACT.Copy,
                                                   scale=NA_SCALE)
                    ins.then_inc(act_drain, 1)
                elif kind == "v":
                    f, h = x["what"]
                    act.wait_ge(gemm_done, g + 1)
                    if f == 1:
                        act.wait_ge(gemm_done, gid("vt", which, 0, 2) + 1)
                    elif which == 1:
                        act.wait_ge(gemm_done, gid("vt", 0, 1, 2) + 1)
                    r0, r1 = (0, 5) if h == 0 else (5, ROWS)
                    flat = vg[:, 0:8, :].rearrange("p a b -> p (a b)")
                    for j in range(NQB):
                        ins = nc.scalar.activation(
                            flat[:, (j * ROWS + r0) * KB:(j * ROWS + r1) * KB].rearrange("p (r k) -> p r k", k=KB),
                            bank[:, 0:(r1 - r0) * GRID].rearrange("p (r c) -> p r c", c=GRID)[
                                :, :, KSTART[j]:KSTART[j] + KB], ACT.Copy)
                    if h == 1:
                        ins = nc.scalar.activation(vg[:, 8, :], bank[:, HT - P:HT], ACT.Copy)
                    ins.then_inc(act_drain, 1)
                elif kind in ("mq", "k", "mk"):
                    dst, sc = dict(mq=(mq, M_SCALE), k=(nak, 1.0), mk=(mk, 1.0))[kind]
                    f, h = x["what"]
                    act.wait_ge(gemm_done, g + 1)
                    nc.scalar.activation(dst[:, 2 * which + f, half(h)], bank, ACT.Copy, scale=sc).then_inc(act_drain, 1)
                elif kind == "mv":
                    f, h = x["what"]
                    act.wait_ge(gemm_done, g + 1)
                    if f == 1:
                        act.wait_ge(gemm_done, gid("mvt", which, 0, 1) + 1)
                    v = vg[:, 0:TT, :].rearrange("p a b -> p (a b)")
                    nc.scalar.activation(v[:, half(h)], bank, ACT.Copy).then_inc(act_drain, 1)
                elif kind == "cc":
                    f, h = x["what"]
                    act.wait_ge(gemm_done, g + 1)
                    act.wait_ge(conv_rd, 2 * which)
                    nc.scalar.activation(cu[:, f, half(h)], bank, ACT.Copy).then_inc(act_drain, 1)
                elif kind == "cb":
                    f, h = x["what"]
                    if h == 1:
                        act.wait_ge(dve_drain, drains("V", g))
                        act.wait_ge(ms_rd, 6)
                        nc.scalar.activation(bo_hi[:, 2 * which + f, :], t1[:, f, :], ACT.Copy).then_inc(bo_hid, 1)
                elif kind == "gate":
                    f, h = x["what"]
                    b, i = which
                    act.wait_ge(gemm_done, g + 1)
                    before = 4 * (4 * (2, 0, 1).index(b) + i)
                    if before:
                        act.wait_ge(merged_add, before)
                    t = 8 * b + 2 * i + f
                    nc.scalar.activation(gt[:, f, half(h)], bank, ACT.Tanh, scale=0.5,
                                         bias=half_bg[:, t:t + 1]).then_inc(act_drain, 1)
                elif kind == "mo":
                    f, h = x["what"]
                    act.wait_ge(gemm_done, g + 1)
                    act.wait_ge(ml_h, len(ML_UNITS))
                    nc.scalar.activation(mo[:, 2 * which + f, half(h)], bank, ACT.Tanh, scale=0.5).then_inc(act_drain, 1)
                elif kind == "ada_row":
                    act.wait_ge(gemm_done, g + 1)
                    nc.scalar.activation(adarow[:, ada_slot(n), :], ps[0:4, x["bank"], 0:UW], ACT.Copy).then_inc(act_drain, 1)
                elif kind == "fg":
                    f, h = x["what"]
                    act.wait_ge(gemm_done, g + 1)
                    if which:
                        act.wait_ge(dve_drain, drains("V", gid("fu", which - 1, f, h)))
                    nc.scalar.activation(sg[:, 2 * f + h, :], bank, ACT.Silu).then_inc(act_drain, 1)
                elif kind in ("out", "down"):
                    c, t = x["what"]
                    full = ps[:, x["bank"], :]
                    act.wait_ge(gemm_done, g + 1)
                    b0, b1, done = (44, 49, y_sq) if kind == "out" else (24, 32, z_sq)
                    col = (b1 if c else b0) + t
                    jk = junk2 if kind == "out" else yb_junk
                    ins = nc.scalar.activation(jk[:, 0:512], full, ACT.Square, accum_out=small[:, col:col + 1])
                    if c == 0:
                        link(ins)
                        dst = x1[:, t, 0:512] if kind == "out" else y2[:, t, :]
                        nc.scalar.activation(dst, full, ACT.Copy).then_inc(act_drain, 1)
                    else:
                        ins.then_inc(done, 1)
                        act.wait_ge(done, t + 1)

            for t in range(TT):
                act.wait_ge(x_in[t], 16)
                nc.scalar.activation(junk[:, :], xt[:, t, :], ACT.Square,
                                     accum_out=small[:, t:t + 1]).then_inc(x_sq, 1)
                act.wait_ge(x_sq, t + 1)
            act.wait_ge(cols_rd, 1)
            link(nc.scalar.activation(sil[:, :], cols[:, R_C:R_C + 16], ACT.Silu))
            nc.scalar.activation(cond[:, :, 0:2], sil[:, :].rearrange("p (c k) -> p k c", c=2), ACT.Copy).then_inc(cond_hi, 1)
            split_hi(0)
            for k in range(1, KD, 2):
                act.wait_ge(xl_tr, k + 1)
                nc.scalar.activation(xnt[:, k, 0:LAT], ps[:, k % 4, :], ACT.Copy).then_inc(xt_act, 1)
            for step in PLAN:
                if step[0] == "unit":
                    n = step[1]
                    if n + 1 < len(UNITS):
                        split_hi(n + 1)
                    if UNITS[n][0] == "down":
                        o = 6 * UNITS[n][1][0] + UNITS[n][1][1]
                        if o < 11:
                            ff_hi(o + 1)
                    if UNITS[n][:2] == ("gate", (0, 0)):
                        branch_hi(att, gid("br", (2, 3), 1, 1), (na_out, len(NA_UNITS)), 4)
                    if UNITS[n][:2] == ("gate", (1, 0)):
                        branch_hi(hmt, gid("br", (0, 3), 1, 1), (hm_out, TT), 8)
                elif step[0] == "group":
                    drain(step[1])
                elif step[0] == "h":
                    for k in (2 * step[1], 2 * step[1] + 1):
                        act.wait_ge(h_aff, k + 1)
                        nc.scalar.activation(h_hi[:, k, :], xnt[:, k, :], ACT.Copy).then_inc(h_hid, 1)
                elif step[0] == "na":
                    _, sub, s = step
                    if sub == 0 and s < len(NA_UNITS):
                        lat = NA_UNITS[s][0] == "lat"
                        act.wait_ge(na_max, s + 1)
                        b = s % 2
                        m = 2 if lat else 4
                        w = NKEY if lat else CTX
                        for i in range(m):
                            v = sx[:, b, i, :] if lat else sx[:, b, i // 2, (i % 2) * CTX:(i % 2 + 1) * CTX]
                            ins = nc.scalar.activation(v, v, ACT.Exp, bias=small[:, 16 + i:17 + i],
                                                       accum_out=small[:, 20 + i:21 + i])
                        ins.then_inc(na_exp, 1)
                        act.wait_ge(na_exp, s + 1)
                    if sub == 1 and 0 <= s - 1 < len(NA_UNITS):
                        n = s - 1
                        w = NKEY if NA_UNITS[n][0] == "lat" else 2 * CTX
                        act.wait_ge(na_tr, n + 1)
                        if n >= 2:
                            act.wait_ge(na_pv, n - 1)
                        nc.scalar.activation(pt[:, n % 2, :, 0:w], ps[:, 6:8, 0:w], ACT.Copy).then_inc(na_pt, 1)
                elif step[0] == "mstat":
                    act.wait_ge(f_neg, 1)
                    nc.scalar.activation(st[1][:, :], st[0][:, :], ACT.Exp).then_inc(f_exp, 1)
                    act.wait_ge(f_exp, 1)
                    nc.scalar.activation(st[2][:, :], st[1][:, :], ACT.Ln, bias=1.0).then_inc(f_ln, 1)
                    act.wait_ge(s_exp_in, 1)
                    for i in (4, 5, 2):
                        ins = nc.scalar.activation(st[i][:, :], st[i][:, :], ACT.Exp)
                    ins.then_inc(s_exp, 1)
                elif step[0] == "ml":
                    _, sub, n = step
                    ch, dr, hp, first, last = ML_UNITS[n]
                    b = n % 2
                    if sub == 0:
                        act.wait_ge(ml_a, n + 1)
                        if n == 0:
                            act.wait_ge(ms_rd, 6)
                        for i in range(2):
                            r = dr * 4 + 2 * hp + i
                            ins = nc.scalar.activation(kw_sb[:, b, i, :], A[2][:, i * P:(i + 1) * P], ACT.Copy,
                                                       scale=mcols[:, ch, 2, r:r + 1])
                        ins.then_inc(ml_kw, 1)
                        act.wait_ge(ml_dm, n + 1)
                        nc.scalar.activation(e_sb[:, b], e_sb[:, b], ACT.Exp, scale=-1.0).then_inc(ml_e, 1)
                    elif ch < CH:
                        act.wait_ge(ml_b, n + 1)
                        for i in range(2):
                            r = dr * 4 + 2 * hp + i
                            ins = nc.scalar.activation(tmp_sb[:, i, :], A[0][:, i * 129:(i + 1) * 129], ACT.Copy,
                                                       scale=mcols[:, ch, 1, r:r + 1])
                        ins.then_inc(ml_tmp, 1)
                elif step[0] == "out_start":
                    act.wait_ge(merged_add, 4 * 12)
                    act.wait_ge(gemm_done, gid("gate", (1, 3), 1, 1) + 1)
                    for k in range(KD):
                        nc.scalar.activation(h_hi[:, k, :], merged[:, k, :], ACT.Copy, scale=0.5).then_inc(mg_hid, 1)
                elif step[0] == "down_start":
                    first_ff_hi(step[1])
                elif step[0] == "square2":
                    t = step[1]
                    act.wait_ge(x1_rd, t + 1)
                    nc.scalar.activation(junk2[:, :], x1[:, t, :], ACT.Square,
                                         accum_out=small[:, 8 + t:9 + t]).then_inc(x1_sq, 1)
                    act.wait_ge(x1_sq, t + 1)
                elif step[0] == "turn2":
                    t = step[1]
                    act.wait_ge(x1_rstd, t + 1)
                    if t >= 2:
                        act.wait_ge(n2_tr, 2 * t - 2)
                    nc.scalar.activation(xn[:, t % 2, :], x1[:, t, :], ACT.Copy,
                                         scale=small[:, 8 + t:9 + t]).then_inc(xn_rd, 1)
                elif step[0] == "split2":
                    t = step[1]
                    act.wait_ge(n2_ev, 2 * t + 2)
                    nc.scalar.activation(h_hi[:, :, tok(t)], h32[:, t % 2], ACT.Copy).then_inc(n2_hid, 1)

        @block.vector
        def _(dve):
            seen = [0]

            def link(ins):
                seen[0] += 1
                ins.then_inc(dve_order, 1)
                dve.wait_ge(dve_order, seen[0])

            def branch_lo(src, k0):
                for k in range(4):
                    dve.wait_ge(bo_hid, k0 + k + 1)
                    nc.vector.tensor_tensor(bo_lo[:, k, :], src[:, k, :], bo_hi[:, k, :].bitcast(F32),
                                            ALU.subtract).then_inc(bo_lod, 1)

            def ff_lo(o):
                i = o % 6
                kc = 4 if i < 5 else 2
                dve.wait_ge(ffs_hi, TT + o)
                o2 = 4 * (o % 2)
                nc.vector.tensor_tensor(h_lo[:, o2:o2 + kc, :], ff[:, 4 * i:4 * i + kc, :],
                                        h_hi[:, o2:o2 + kc, :].bitcast(F32), ALU.subtract).then_inc(ffs_lo, 1)

            def drain(g):
                x = GROUPS[g]
                if x["eng"] != "V":
                    return
                kind, n = x["kind"], x["unit"]
                which = UNITS[n][1]
                full = ps[:, x["bank"], :]
                bank = full[:, 0:HT]
                if kind in ("out", "down"):
                    return
                dve.wait_ge(gemm_done, g + 1)
                if kind == "vt":
                    f, c = x["what"]
                    ft = 2 * which + f
                    if c < 2:
                        nc.vector.tensor_copy(vtok[:, 4 * c:4 * c + 4, tok(ft)],
                                              full.rearrange("p (a b) -> p a b", a=4)).then_inc(dve_drain, 1)
                    else:
                        nc.vector.tensor_copy(vtok[:, 8, tok(ft)], full[:, 0:P]).then_inc(dve_drain, 1)
                elif kind == "mvt":
                    f, c = x["what"]
                    ft = 2 * which + f
                    if c == 0:
                        nc.vector.tensor_copy(mv[:, 0:CH, ft, 0:128],
                                              full.rearrange("p (a b) -> p a b", a=4)).then_inc(dve_drain, 1)
                    else:
                        nc.vector.tensor_copy(mv[:, CH, ft, 0:128], full[:, 0:P]).then_inc(dve_drain, 1)
                elif kind == "kout":
                    nc.vector.tensor_copy(sx[:, 0, :, :].rearrange("p a k -> p (a k)")[:, 0:512], full).then_inc(dve_drain, 1)
                elif kind == "mif":
                    f, h = x["what"]
                    dve.wait_ge(gb_in, 16)
                    link(nc.vector.tensor_scalar(ib[:, half(h)], bank[0:RW], gbias[:, 0:1], None, ALU.add))
                    nc.vector.tensor_scalar(lf[:, half(h)], bank[64:64 + RW], gbias[:, 1:2], None,
                                            ALU.add).then_inc(dve_drain, 1)
                elif kind == "cx":
                    f, h = x["what"]
                    dve.wait_ge(act_drain, drains("A", gid("cc", which, f, h)))
                    v = cu[:, f, half(h)]
                    nc.vector.tensor_tensor(v, bank, v, ALU.mult).then_inc(dve_drain, 1)
                    if h == 1:
                        dve.wait_ge(dve_drain, drains("V", g))
                        if which:
                            dve.wait_ge(bo_lod, f + 1)
                        ft = 2 * which + f
                        w = [cols[:, R_CW + 4 * k + ft:R_CW + 4 * k + ft + 1] for k in range(3)]
                        u, y = cu[:, f, :], t1[:, f, :]
                        link(nc.vector.tensor_scalar(y, u, w[1], None, ALU.mult))
                        parts = []
                        for lo, hi in ((0, LAT), (LAT, T)):
                            parts += [(lo + 1, hi, -1, w[0]), (lo, hi - 1, 1, w[2])]
                        for j, (lo, hi, d, wk) in enumerate(parts):
                            ins = nc.vector.scalar_tensor_tensor(y[:, lo:hi], u[:, lo + d:hi + d], wk, y[:, lo:hi],
                                                                 ALU.mult, ALU.add)
                            if j < 3:
                                link(ins)
                        ins.then_inc(conv_rd, 1)
                elif kind == "cb":
                    f, h = x["what"]
                    dve.wait_ge(conv_rd, 2 * which + f + 1)
                    v = t1[:, f, half(h)]
                    nc.vector.tensor_tensor(v, bank, v, ALU.mult).then_inc(dve_drain, 1)
                    if h == 1:
                        k = 2 * which + f
                        dve.wait_ge(bo_hid, k + 1)
                        nc.vector.tensor_tensor(bo_lo[:, k, :], t1[:, f, :], bo_hi[:, k, :].bitcast(F32),
                                                ALU.subtract).then_inc(bo_lod, 1)
                elif kind == "br":
                    f, h = x["what"]
                    b, i = which
                    dve.wait_ge(act_drain, drains("A", gid("gate", which, f, h)))
                    v = gt[:, f, half(h)]
                    mg = merged[:, 2 * i + f, half(h)]
                    nc.vector.scalar_tensor_tensor(v, v, 1.0, bank, ALU.add, ALU.mult).then_inc(dve_drain, 1)
                    dve.wait_ge(dve_drain, drains("V", g))
                    if b == 2:
                        nc.vector.tensor_copy(mg, v).then_inc(merged_add, 1)
                    else:
                        nc.vector.tensor_tensor(mg, mg, v, ALU.add).then_inc(merged_add, 1)
                elif kind == "ada_col":
                    m, i = which
                    if m in (2, 5):
                        gd, bb, landed = (g1, bb1, bc1_in) if m == 2 else (g2, bb2, bc2_in)
                        dve.wait_ge(landed, 32)
                        if m == 5:
                            for s in c_out:
                                dve.wait_ge(s, 64)
                        cc = slice(i * UW, (i + 1) * UW)
                        v = gd[:, :, cc]
                        nc.vector.tensor_tensor(v, full.rearrange("p (c w) -> p c w", c=2),
                                                bb[:, 0:1, cc].to_broadcast([P, 2, UW]), ALU.add).then_inc(dve_drain, 1)
                        dve.wait_ge(dve_drain, drains("V", g))
                        link(nc.vector.tensor_tensor(v, v, bb[:, 1:2, cc].to_broadcast([P, 2, UW]), ALU.mult))
                    else:
                        j = {1: 0, 0: 1, 4: 2, 3: 3}[m]
                        v = mod[:, j, 2 * i:2 * i + 2, :]
                        bc = cols[:, R_BADA + 8 * m + 2 * i:R_BADA + 8 * m + 2 * i + 2]
                        nc.vector.tensor_tensor(v, full[:, 0:4].rearrange("p (k c) -> p k c", k=2),
                                                bc.unsqueeze(2).to_broadcast([P, 2, 2]), ALU.add).then_inc(dve_drain, 1)
                        dve.wait_ge(dve_drain, drains("V", g))
                        if m in (1, 4):
                            r = (R_GPM if m == 1 else R_GPF) + 2 * i
                            link(nc.vector.scalar_tensor_tensor(
                                v, v, 1.0, cols[:, r:r + 2].unsqueeze(2).to_broadcast([P, 2, 2]), ALU.add, ALU.mult))
                elif kind == "fu":
                    f, h = x["what"]
                    dve.wait_ge(act_drain, drains("A", gid("fg", which, f, h)))
                    nc.vector.tensor_tensor(ff[:, 2 * which + f, half(h)], bank, sg[:, 2 * f + h, :],
                                            ALU.mult).then_inc(dve_drain, 1)

            dve.wait_ge(cols_tr, 1)
            nc.vector.tensor_copy(cols[:, :], A[0][:, 0:NROWS]).then_inc(cols_rd, 1)
            dve.wait_ge(cols_rd, 1)
            link(nc.vector.tensor_scalar(half_bg[:, :], cols[:, R_BG:R_BG + 24], 0.5, None, ALU.mult))
            dve.wait_ge(kc_tr, 1)
            nc.vector.tensor_copy(kct[:, :, :], A[1].rearrange("p (a b) -> p a b", a=4)).then_inc(kc_rd, 1)
            dve.wait_ge(cond_hi, 1)
            nc.vector.tensor_tensor(cond[:, :, 2:4], sil[:, :].rearrange("p (c k) -> p k c", c=2),
                                    cond[:, :, 0:2].bitcast(F32), ALU.subtract).then_inc(cond_rd, 1)
            dve.wait_ge(x_rstd, 1)
            for t in range(TT):
                nc.vector.tensor_scalar(xt[:, t, :], xt[:, t, :], small[:, 8 + t:9 + t], None,
                                        ALU.mult).then_inc(x_nrm, 1)
            split_low(nc.vector, dve, 0)
            for k in range(0, KD, 2):
                dve.wait_ge(xl_tr, k + 1)
                nc.vector.tensor_copy(xnt[:, k, 0:LAT], ps[:, k % 4, :]).then_inc(xt_dve, 1)
            for i in range(2):
                dve.wait_ge(xc_tr, i + 1)
                nc.vector.tensor_copy(xnt[:, 4 * i:4 * i + 4, LAT:T],
                                      A[2 + i].rearrange("p (a b) -> p a b", a=4)).then_inc(xc_dve, 1)
            written = set()
            for step in PLAN:
                if step[0] == "unit":
                    n = step[1]
                    if n + 1 < len(UNITS) and lo_engine(n + 1) == "V":
                        split_low(nc.vector, dve, n + 1)
                    if UNITS[n][0] == "down":
                        o = 6 * UNITS[n][1][0] + UNITS[n][1][1]
                        if o < 11:
                            ff_lo(o + 1)
                    if UNITS[n][:2] == ("gate", (0, 0)):
                        branch_lo(att, 4)
                    if UNITS[n][:2] == ("gate", (1, 0)):
                        branch_lo(hmt, 8)
                elif step[0] == "group":
                    drain(step[1])
                elif step[0] == "h":
                    if step[1] == 0:
                        dve.wait_ge(xt_act, 4)
                        dve.wait_ge(xt_dve, 4)
                        dve.wait_ge(xc_dve, 2)
                    for k in (2 * step[1], 2 * step[1] + 1):
                        for c, sl in ((0, slice(0, LAT)), (1, slice(LAT, T))):
                            ins = nc.vector.tensor_scalar(xnt[:, k, sl], xnt[:, k, sl], mod[:, 0, k, c:c + 1],
                                                          mod[:, 1, k, c:c + 1], ALU.mult, ALU.add)
                        ins.then_inc(h_aff, 1)
                    for k in (2 * step[1], 2 * step[1] + 1):
                        dve.wait_ge(h_hid, k + 1)
                        nc.vector.tensor_tensor(h_lo[:, k, :], xnt[:, k, :], h_hi[:, k, :].bitcast(F32),
                                                ALU.subtract).then_inc(h_lod, 1)
                elif step[0] == "na":
                    _, sub, s = step
                    if sub == 0:
                        n = s - 2
                        if 0 <= n < len(NA_UNITS):
                            kind, hp, j = NA_UNITS[n]
                            dve.wait_ge(na_pv, n + 1)
                            if kind == "lat":
                                v = att[:, hp, 0:LAT].rearrange("p (r c) -> p r c", c=GRID)[:, :, j * QB:(j + 1) * QB]
                                nc.vector.tensor_copy(v, A[3][:, NKEY:512].rearrange("p (r c) -> p r c", r=ROWS)[:, :, ::-1]
                                                      ).then_inc(na_out, 1)
                            else:
                                nc.vector.tensor_copy(att[:, 2 * hp:2 * hp + 2, LAT:T],
                                                      A[3][:, 256:512].rearrange("p (i t) -> p i t", i=2)
                                                      ).then_inc(na_out, 1)
                        if s < len(NA_UNITS):
                            kind, hp, j = NA_UNITS[s]
                            b = s % 2
                            dve.wait_ge(na_sc, s + 1)
                            if s >= 2:
                                dve.wait_ge(na_tr, s - 1)
                            if kind == "lat":
                                if s == 0:
                                    dve.wait_ge(bias_zero, 1)
                                dve.wait_ge(bias_rd, 3 * hp + BTYPE[j] + 1)
                                nc.vector.tensor_tensor(sx[:, b], ps[:, 4:6, 0:NKEY], bm[:, BTYPE[j]],
                                                        ALU.add).then_inc(na_add, 1)
                                dve.wait_ge(na_add, s + 1)
                                nc.vector.tensor_reduce(small[:, 16:18], sx[:, b], X, ALU.max, negate=True).then_inc(na_max, 1)
                            else:
                                v = sx[:, b, :, 0:256]
                                nc.vector.tensor_copy(v, ps[:, 4:6, 0:256]).then_inc(na_add, 1)
                                dve.wait_ge(na_add, s + 1)
                                nc.vector.tensor_reduce(small[:, 16:20].rearrange("p (a i) -> p a i", a=2),
                                                        v.rearrange("p a (i k) -> p a i k", i=2), X, ALU.max,
                                                        negate=True).then_inc(na_max, 1)
                    if sub == 1 and s < len(NA_UNITS):
                        kind, hp, j = NA_UNITS[s]
                        b = s % 2
                        m = 2 if kind == "lat" else 4
                        dve.wait_ge(na_exp, s + 1)
                        link(nc.vector.reciprocal(small[:, 24:24 + m], small[:, 20:20 + m]))
                        for i in range(m):
                            v = sx[:, b, i, :] if m == 2 else sx[:, b, i // 2, (i % 2) * CTX:(i % 2 + 1) * CTX]
                            ins = nc.vector.tensor_scalar(v, v, small[:, 24 + i:25 + i], None, ALU.mult)
                        ins.then_inc(na_prob, 1)
                        dve.wait_ge(na_prob, s + 1)
                elif step[0] == "mstat":
                    dve.wait_ge(dve_drain, drains("V", gid("mif", 0, 0, 1)))
                    nc.vector.scalar_tensor_tensor(st[0][:, :], lf[:, :], -1.0, lf[:, :], ALU.mult,
                                                   ALU.min).then_inc(f_neg, 1)
                    dve.wait_ge(f_ln, 1)
                    link(nc.vector.scalar_tensor_tensor(lf[:, :], lf[:, :], 0.0, st[2][:, :], ALU.min, ALU.subtract))
                    spans = ((0, LAT), (LAT, T))

                    def turned(dst, src):
                        nc.vector.tensor_copy(dst[0:32, :], src[0:32, :])
                        for lo, hi in spans:
                            ins = nc.vector.tensor_copy(dst[32:RW, lo:hi], src[32:RW, lo:hi][:, ::-1])
                        return ins

                    link(turned(st[0], ib))
                    link(turned(st[1], lf))
                    ones, zero, m0 = st[6], small[0:RW, 42:43], gbias[:, 2:3]
                    link(nc.vector.memset(ones[:, :], 1.0))
                    link(nc.vector.memset(zero, 0.0))
                    for c in range(TT):
                        ins = nc.vector.tensor_tensor_scan(st[2][:, tok(c)], ones[:, tok(c)], st[1][:, tok(c)], 0.0,
                                                           ALU.mult, ALU.add)
                    link(ins)
                    link(nc.vector.tensor_tensor(st[0][:, :], st[0][:, :], st[2][:, :], ALU.subtract))
                    mcur = m0
                    for c in range(TT):
                        if c == CH:
                            mcur = zero
                        end = (c + 1) * P
                        link(nc.vector.tensor_tensor_scan(st[3][:, tok(c)], st[0][:, tok(c)], st[0][:, tok(c)], mcur,
                                                          ALU.max, ALU.max))
                        nc.vector.tensor_scalar(st[4][:, tok(c)], st[3][:, tok(c)], -1.0, mcur, ALU.mult, ALU.add)
                        nc.vector.tensor_scalar(st[5][:, tok(c)], st[0][:, tok(c)], st[3][:, end - 1:end], None,
                                                ALU.subtract)
                        nxt = small[0:RW, 57 + c:58 + c] if c < CH else small[0:RW, 40:41]
                        ins = nc.vector.tensor_tensor(nxt, st[2][:, end - 1:end], st[3][:, end - 1:end], ALU.add)
                        if c == CH:
                            ins.then_inc(m_fin, 1)
                            dve.wait_ge(m_fin, 1)
                        else:
                            link(ins)
                        mcur = nxt
                    nc.vector.scalar_tensor_tensor(st[2][:, :], st[2][:, :], -1.0, st[3][:, :], ALU.mult,
                                                   ALU.subtract).then_inc(s_exp_in, 1)
                    dve.wait_ge(s_exp_in, 1)
                    dve.wait_ge(stored, 32)
                    turned(ib, st[0])
                    link(turned(mnat, st[3]))
                    dve.wait_ge(s_exp, 1)
                    turned(lf, st[4])
                    turned(st[1], st[5])
                    turned(st[6], st[2]).then_inc(nat_rd, 1)
                elif step[0] == "mcols":
                    for c in range(TT):
                        dve.wait_ge(ms_tr, c + 1)
                        src = A[c % 2][:, 0:4 * RW].rearrange("p (q r) -> p q r", q=4)
                        nc.vector.tensor_copy(mcols[:, c, :, 0:4], src[:, :, 0:4])
                        nc.vector.tensor_copy(mcols[:, c, :, 4:8], src[:, :, 32:36]).then_inc(ms_rd, 1)
                    dve.wait_ge(ms_tr, TT + 1)
                    nc.vector.tensor_copy(dec[:, :, :], A[2][:, 0:32].rearrange("p (r c) -> p r c", r=8)).then_inc(ms_rd, 1)
                    dve.wait_ge(ms_rd, 6)
                    dve.wait_ge(state_in, 32)
                elif step[0] == "ml":
                    _, sub, n = step
                    ch, dr, hp, first, last = ML_UNITS[n]
                    b = n % 2
                    if sub == 0:
                        dve.wait_ge(ml_a, n + 1)
                        for i in range(2):
                            r = dr * 4 + 2 * hp + i
                            ins = nc.vector.scalar_tensor_tensor(e_sb[:, b, i, :], A[0][:, i * P:(i + 1) * P],
                                                                 mcols[:, ch, 0, r:r + 1], mask_m[:, dr, :],
                                                                 ALU.subtract, ALU.max)
                        ins.then_inc(ml_dm, 1)
                        dve.wait_ge(ml_e, n + 1)
                        nc.vector.tensor_tensor(st_sb[:, b], A[1][:, 0:256].rearrange("p (i t) -> p i t", i=2),
                                                e_sb[:, b], ALU.mult).then_inc(ml_st, 1)
                    else:
                        dve.wait_ge(ml_b, n + 1)
                        intra = A[3][:, 0:258].rearrange("p (i e) -> p i e", i=2)
                        upd = A[1][:, 0:258].rearrange("p (i e) -> p i e", i=2)
                        if ch < CH:
                            dve.wait_ge(ml_tmp, n - 3)
                            ins = nc.vector.tensor_tensor(num_sb[:, :, :], intra, tmp_sb[:, :, :], ALU.add)
                            if not last:
                                link(ins)
                                for i in range(2):
                                    r = dr * 4 + 2 * hp + i
                                    ins = nc.vector.scalar_tensor_tensor(cl[:, r, :], cl[:, r, :], dec[:, r, ch:ch + 1],
                                                                         upd[:, i, :], ALU.mult, ALU.add)
                        else:
                            link(nc.vector.tensor_copy(num_sb[:, :, :], intra))
                            if n >= 2:
                                dve.wait_ge(c_out[n % 2], 32)
                            ins = nc.vector.tensor_copy(cout[:, n % 2], upd)
                        ins.then_inc(ml_c, 1)
                        dve.wait_ge(ml_c, n + 1)
                        den = num_sb[:, :, 128]
                        d = small[:, 24:26]
                        r0 = dr * 4 + 2 * hp
                        link(nc.vector.scalar_tensor_tensor(d, den, -1.0, den, ALU.mult, ALU.max))
                        link(nc.vector.tensor_tensor(d, d, mcols[:, ch, 3, r0:r0 + 2], ALU.max))
                        link(nc.vector.reciprocal(d, d))
                        for i in range(2):
                            hd = 2 * hp + i
                            v = hsum[:, ch, hd * 128:(hd + 1) * 128]
                            if (ch, hd) in written:
                                ins = nc.vector.scalar_tensor_tensor(v, num_sb[:, i, 0:128], d[:, i:i + 1], v,
                                                                     ALU.mult, ALU.add)
                            else:
                                ins = nc.vector.tensor_scalar(v, num_sb[:, i, 0:128], d[:, i:i + 1], None, ALU.mult)
                            written.add((ch, hd))
                        ins.then_inc(ml_h, 1)
                        dve.wait_ge(ml_h, n + 1)
                elif step[0] == "hm":
                    _, sub, c = step
                    v = small[:, 16 + 4 * c:20 + 4 * c] if c < 4 else small[:, 32:36]
                    if sub == 0:
                        sq = st_sb[:, :, :, :].rearrange("p a b c -> p (a b c)")
                        link(nc.vector.tensor_tensor(sq, hsum[:, c, :], hsum[:, c, :], ALU.mult))
                        nc.vector.tensor_reduce(v, sq.rearrange("p (h d) -> p h d", h=MH), X, ALU.add).then_inc(hm_sq, 1)
                        dve.wait_ge(hm_sq, c + 1)
                    else:
                        dve.wait_ge(hm_rstd, c + 1)
                        y = hsum[:, c, :].rearrange("p (h d) -> p h d", h=MH)
                        nc.vector.tensor_tensor(y, y, v.unsqueeze(2).to_broadcast([P, MH, 128]), ALU.mult).then_inc(hm_nrm, 1)
                        dve.wait_ge(hm_tr, c + 1)
                        dve.wait_ge(mo_rd, 8)
                        for hd in range(MH):
                            ins = nc.vector.scalar_tensor_tensor(
                                hmt[:, hd, tok(c)], A[c % 4][:, hd * P:(hd + 1) * P],
                                cols[:, R_MG + hd:R_MG + hd + 1], mo[:, hd, tok(c)], ALU.mult, ALU.mult)
                        ins.then_inc(hm_out, 1)
                elif step[0] == "out_start":
                    for k in range(KD):
                        dve.wait_ge(mg_hid, k + 1)
                        nc.vector.scalar_tensor_tensor(h_lo[:, k, :], merged[:, k, :], 0.5,
                                                       h_hi[:, k, :].bitcast(F32), ALU.mult,
                                                       ALU.subtract).then_inc(mg_lod, 1)
                elif step[0] == "down_start":
                    t = step[1]
                    dve.wait_ge(ffs_hi, t + 1)
                    nc.vector.tensor_tensor(h_lo[:, 0:4, tok(t)], ff[:, 0:4, tok(t)],
                                            h_hi[:, 0:4, tok(t)].bitcast(F32), ALU.subtract).then_inc(ffs_lo, 1)
                elif step[0] == "resid":
                    t = step[1]
                    cnd = 0 if t < CH else 1
                    g = gid("out", (1, 1), 1, t)
                    dve.wait_ge(y_rstd, t + 1)
                    dve.wait_ge(act_drain, drains("A", gid("out", (0, 1), 0, t)))
                    r = small[:, t:t + 1]
                    nc.vector.scalar_tensor_tensor(x1[:, t, 0:512], x1[:, t, 0:512], r, g1[:, cnd, 0:512],
                                                   ALU.mult, ALU.mult)
                    nc.vector.scalar_tensor_tensor(x1[:, t, 512:D], ps[:, GROUPS[g]["bank"], :], r,
                                                   g1[:, cnd, 512:D], ALU.mult, ALU.mult).then_inc(dve_drain, 1)
                    dve.wait_ge(dve_drain, drains("V", g))
                    dve.wait_ge(xb_in[t % 2], 16 * (t // 2 + 1))
                    nc.vector.tensor_tensor(x1[:, t, :], x1[:, t, :], xb[:, t % 2, :], ALU.add).then_inc(x1_rd, 1)
                elif step[0] == "turn2":
                    t = step[1]
                    cnd = 0 if t < CH else 1
                    for hh in range(2):
                        dve.wait_ge(n2_tr, 2 * t + hh + 1)
                        if t >= 2:
                            dve.wait_ge(n2_lod, t - 1)
                        b = 2 + (2 * t + hh) % 3
                        for kk in range(4):
                            k = 4 * hh + kk
                            ins = nc.vector.tensor_scalar(h32[:, t % 2, k, :], ps[:, b, kk * P:(kk + 1) * P],
                                                          mod[:, 2, k, cnd:cnd + 1], mod[:, 3, k, cnd:cnd + 1],
                                                          ALU.mult, ALU.add)
                        ins.then_inc(n2_ev, 1)
                elif step[0] == "split2":
                    t = step[1]
                    dve.wait_ge(n2_hid, t + 1)
                    nc.vector.tensor_tensor(h_lo[:, :, tok(t)], h32[:, t % 2], h_hi[:, :, tok(t)].bitcast(F32),
                                            ALU.subtract).then_inc(n2_lod, 1)
                elif step[0] == "final":
                    t = step[1]
                    cnd = 0 if t < CH else 1
                    g = gid("down", (1, 5), 1, t)
                    dve.wait_ge(z_rstd, t + 1)
                    dve.wait_ge(act_drain, drains("A", gid("down", (0, 5), 0, t)))
                    r = small[:, 16 + t:17 + t]
                    nc.vector.scalar_tensor_tensor(y2[:, t, :], y2[:, t, :], r, g2[:, cnd, 0:512], ALU.mult, ALU.mult)
                    nc.vector.scalar_tensor_tensor(yb[:, :], ps[:, GROUPS[g]["bank"], :], r, g2[:, cnd, 512:D],
                                                   ALU.mult, ALU.mult).then_inc(dve_drain, 1)
                    dve.wait_ge(dve_drain, drains("V", g))
                    nc.vector.tensor_tensor(x1[:, t, 0:512], x1[:, t, 0:512], y2[:, t, :], ALU.add)
                    nc.vector.tensor_tensor(x1[:, t, 512:D], x1[:, t, 512:D], yb[:, :], ALU.add).then_inc(fin_rd, 1)
                    dve.wait_ge(fin_rd, t + 1)

        @block.tensor
        def _(pe):
            def bank_free(g):
                prev = last_user(GROUPS[g]["bank"], g)
                if prev is not None:
                    e = GROUPS[prev]["eng"]
                    pe.wait_ge(act_drain if e == "A" else dve_drain, drains(e, prev))

            def three(dst, wh, wl, xh, xl, first, last):
                nc.tensor.matmul(dst, wh, xh, start=first, stop=False)
                nc.tensor.matmul(dst, wh, xl, start=False, stop=False)
                return nc.tensor.matmul(dst, wl, xh, start=False, stop=last)

            def unit_ready(n):
                pe.wait_ge(hi_done, n + 1)
                wait_lo(pe, n)

            def group(g):
                x = GROUPS[g]
                kind, n, what = x["kind"], x["unit"], x["what"]
                which = UNITS[n][1]
                full = ps[:, x["bank"], :]
                if kind not in ("out", "down"):
                    bank_free(g)
                if kind == "ada_row":
                    wh, wl = slot(w_hi, n), slot(w_lo, n)
                    for k in range(KD):
                        nc.tensor.matmul(full[0:4, 0:UW], cond[:, k, :], wh[:, k, :], start=(k == 0), stop=False)
                        ins = nc.tensor.matmul(full[0:4, 0:UW], cond[:, k, :], wl[:, k, :], start=False,
                                               stop=(k == KD - 1))
                elif kind == "ada_col":
                    m = which[0]
                    rowg = next(i for i in range(g - 1, -1, -1) if GROUPS[i]["kind"] == "ada_row" and GROUPS[i]["unit"] == n)
                    pe.wait_ge(act_drain, drains("A", rowg))
                    ar = adarow[:, ada_slot(n), :]
                    if m in (2, 5):
                        for c in range(2):
                            ins = nc.tensor.matmul(full[:, c * UW:(c + 1) * UW], sel[:, c, :], ar, start=True, stop=True)
                    else:
                        for k in range(2):
                            ins = nc.tensor.matmul(full[:, 2 * k:2 * k + 2], ar[:, k * P:(k + 1) * P], sel[:, :, 0],
                                                   start=True, stop=True)
                elif kind == "vt":
                    f, c = what
                    pe.wait_ge(act_drain, drains("A", gid("v", which, f, 1)))
                    for i in range(4 if c < 2 else 1):
                        ins = nc.tensor.transpose(full[:, i * P:(i + 1) * P], vg[:, 4 * c + i, :], ident)
                elif kind == "mvt":
                    f, c = what
                    pe.wait_ge(act_drain, drains("A", gid("mv", which, f, 1)))
                    for i in range(4 if c == 0 else 1):
                        ins = nc.tensor.transpose(full[:, i * P:(i + 1) * P], vg[:, 4 * c + i, :], ident)
                elif kind == "kout":
                    for i in range(4):
                        ins = nc.tensor.transpose(full[:, i * P:(i + 1) * P], nak[:, i, LAT:T], ident)
                elif kind in ("out", "down"):
                    part(kind, what[0], what[1], 1 if kind == "out" else 5).then_inc(gemm_done, 1)
                    return
                else:
                    f, h = what
                    wh, wl = slot(w_hi, n), slot(w_lo, n)
                    if kind in ("fg", "fu") and which == 0:
                        pe.wait_ge(n2_lod, 3 if h == 0 else TT)
                    for k in range(UNITS[n][2]):
                        if kind == "br":
                            xh, xl = bo_hi, bo_lo
                            pe.wait_ge(bo_lod, 4 * (2, 0, 1).index(which[0]) + k + 1)
                        else:
                            xh, xl = h_hi, h_lo
                            if n == 8:
                                pe.wait_ge(h_lod, k + 1)
                        fs = slice(f * P, (f + 1) * P)
                        ins = three(full[:, 0:HT], wh[:, k, fs], wl[:, k, fs], xh[:, k, half(h)], xl[:, k, half(h)],
                                    k == 0, k == UNITS[n][2] - 1)
                ins.then_inc(gemm_done, 1)

            def part(kind, c, t, i):
                n = UNIT_OF[(kind, (c, i))]
                g = gid(kind, (c, 1 if kind == "out" else 5), c, t)
                if i == 0:
                    bank_free(g)
                wh, wl = slot(w_hi, n), slot(w_lo, n)
                kc = UNITS[n][2]
                dst = ps[:, GROUPS[g]["bank"], :]
                lastu = i == (1 if kind == "out" else 5)
                for k in range(kc):
                    if kind == "out":
                        kk = 4 * i + k
                        if c == 0 and t == 0:
                            pe.wait_ge(mg_lod, kk + 1)
                    else:
                        o = 6 * c + i
                        if k == 0 and o == 0:
                            pe.wait_ge(ffs_lo, t + 1)
                        elif k == 0 and t == 0:
                            pe.wait_ge(ffs_lo, TT + o)
                        kk = 4 * (o % 2) + k
                    ins = three(dst, h_hi[:, kk, tok(t)], h_lo[:, kk, tok(t)], wh[:, k, :], wl[:, k, :],
                                i == 0 and k == 0, lastu and k == kc - 1)
                return ins

            pe.wait_ge(const_in, 16)
            pe.wait_ge(rows_in, 16)
            nc.tensor.transpose(A[0][:, 0:NROWS], rows[:, :], ident[0:NROWS, 0:NROWS]).then_inc(cols_tr, 1)
            pe.wait_ge(kc_in, 16)
            for i in range(4):
                ins = nc.tensor.transpose(A[1][:, i * P:(i + 1) * P], kcr[:, i * P:(i + 1) * P], ident)
            ins.then_inc(kc_tr, 1)
            pe.wait_ge(x_nrm, TT)
            for k in range(KD):
                if k >= 4:
                    pe.wait_ge(xt_act if k % 2 else xt_dve, (k - 4) // 2 + 1)
                for t in range(CH):
                    ins = nc.tensor.transpose(ps[:, k % 4, t * P:(t + 1) * P], xt[:, t, tok(k)], ident)
                ins.then_inc(xl_tr, 1)
            for k in range(KD):
                ins = nc.tensor.transpose(A[2 + k // 4][:, (k % 4) * P:(k % 4 + 1) * P], xt[:, CH, tok(k)], ident)
                if k % 4 == 3:
                    ins.then_inc(xc_tr, 1)
            pe.wait_ge(cond_rd, 1)
            pe.wait_ge(xt_act, 4)
            pe.wait_ge(xt_dve, 4)
            for step in PLAN:
                if step[0] == "unit":
                    unit_ready(step[1])
                elif step[0] == "group":
                    group(step[1])
                elif step[0] == "part":
                    part(step[1], step[2], step[3], step[4] if len(step) > 4 else 0).then_inc(part_done, 1)
                elif step[0] == "na":
                    _, sub, s = step
                    if sub == 0:
                        n = s - 2
                        if 0 <= n < len(NA_UNITS):
                            kind, hp, j = NA_UNITS[n]
                            pe.wait_ge(na_pt, n + 1)
                            if n == 0:
                                pe.wait_ge(vc_in, 16)
                            last_v = gid("vt", 0 if (hp < 2 if kind == "lat" else hp == 0) else 1, 1, 2)
                            pe.wait_ge(dve_drain, drains("V", last_v))
                            for i in range(2):
                                dst = A[3][64 * i:64 * i + 64, :]
                                if kind == "lat":
                                    hc = slice((2 * hp + i) * DH, (2 * hp + i + 1) * DH)
                                    for c in range(3):
                                        src = vtok[:, 2 * j + c, hc] if c < 2 else vtok[:, 9, hc]
                                        ins = nc.tensor.matmul(dst[:, NKEY:512], src, pt[:, n % 2, i, c * P:(c + 1) * P],
                                                               start=(c == 0), stop=(c == 2))
                                else:
                                    for q in range(2):
                                        hd = 2 * (2 * hp + q) + i
                                        ins = nc.tensor.matmul(dst[:, 256 + q * P:256 + (q + 1) * P],
                                                               vtok[:, 8, hd * DH:(hd + 1) * DH],
                                                               pt[:, n % 2, i, q * P:(q + 1) * P], start=True, stop=True)
                            ins.then_inc(na_pv, 1)
                        if s < len(NA_UNITS):
                            kind, hp, j = NA_UNITS[s]
                            p = (hp if kind == "lat" else 2 * hp) // 2
                            pe.wait_ge(act_drain, drains("A", gid("k", p, 1, 1)))
                            if s:
                                pe.wait_ge(na_add, s)
                            else:
                                pe.wait_ge(kc_rd, 1)
                            for i in range(2):
                                pp = slice(64 * i, 64 * i + 64)
                                if kind == "lat":
                                    q = naq[pp, hp, j * P:(j + 1) * P]
                                    kk = nak[pp, hp, 0:LAT].rearrange("p (r c) -> p r c", c=GRID)[
                                        :, :, KSTART[j]:KSTART[j] + KB]
                                    nc.tensor.matmul(A[i][:, 0:256], q, kk, start=True, stop=True)
                                    ins = nc.tensor.matmul(A[i][:, 256:NKEY], q, kct[pp, hp, :], start=True, stop=True)
                                else:
                                    for c in range(2):
                                        ins = nc.tensor.matmul(A[i][:, c * P:(c + 1) * P], naq[pp, 2 * hp + c, LAT:T],
                                                               nak[pp, 2 * hp + c, LAT:T], start=True, stop=True)
                            ins.then_inc(na_sc, 1)
                    if sub == 1 and 0 <= s - 1 < len(NA_UNITS):
                        n = s - 1
                        kind = NA_UNITS[n][0]
                        pe.wait_ge(na_prob, n + 1)
                        if n:
                            pe.wait_ge(na_out, n)
                            pe.wait_ge(na_pt, n)
                        else:
                            pe.wait_ge(xc_dve, 2)
                        for i in range(2):
                            for c in range(3 if kind == "lat" else 2):
                                ins = nc.tensor.transpose(A[2 + i][:, c * P:(c + 1) * P],
                                                          sx[:, n % 2, i, c * P:(c + 1) * P], ident)
                        ins.then_inc(na_tr, 1)
                elif step[0] == "mcols":
                    pe.wait_ge(nat_rd, 1)
                    for c in range(TT):
                        if c >= 2:
                            pe.wait_ge(ms_rd, c - 1)
                        for q, src in enumerate((ib, lf, st[1], st[6])):
                            ins = nc.tensor.transpose(A[c % 2][:, q * RW:(q + 1) * RW], src[:, tok(c)],
                                                      ident[0:RW, 0:RW])
                        ins.then_inc(ms_tr, 1)
                    for dr in range(2):
                        for hd in range(MH):
                            r = dr * 4 + hd
                            sr = dr * 32 + hd
                            e0 = P - 1 if dr == 0 else 0
                            ins = nc.tensor.matmul(A[2][:, r * CH:(r + 1) * CH],
                                                   ident[0:RW, sr:sr + 1].to_broadcast([RW, P]),
                                                   lf[:, e0:e0 + (CH - 1) * P + 1:P], start=True, stop=True)
                    ins.then_inc(ms_tr, 1)
                elif step[0] == "ml":
                    _, sub, n = step
                    ch, dr, hp, first, last = ML_UNITS[n]
                    b = n % 2
                    if sub == 0:
                        pe.wait_ge(ms_rd, 6)
                        if n:
                            pe.wait_ge(ml_c, n)
                        for i in range(2):
                            hd = 2 * hp + i
                            sr = dr * 32 + hd
                            pr = slice(i * P, (i + 1) * P)
                            nc.tensor.matmul(A[0][:, pr], ident[0:RW, sr:sr + 1].to_broadcast([RW, P]),
                                             mnat[:, tok(ch)], start=True, stop=True)
                            nc.tensor.matmul(A[1][:, pr], mk[:, hd, tok(ch)], mq[:, hd, tok(ch)], start=True, stop=True)
                            ins = nc.tensor.transpose(A[2][:, pr], mk[:, hd, tok(ch)], ident)
                        ins.then_inc(ml_a, 1)
                    else:
                        pe.wait_ge(ml_st, n + 1)
                        pe.wait_ge(ml_kw, n + 1)
                        if n == 0:
                            pe.wait_ge(mv_ones, 1)
                            pe.wait_ge(dve_drain, drains("V", gid("mvt", 1, 1, 1)))
                        for i in range(2):
                            hd = 2 * hp + i
                            r = dr * 4 + hd
                            pr = slice(i * 129, (i + 1) * 129)
                            ins = nc.tensor.matmul(A[3][:, pr], st_sb[:, b, i, :], mv[:, ch, hd, :], start=True, stop=True)
                            if ch < CH:
                                ins = nc.tensor.matmul(A[0][:, pr], mq[:, hd, tok(ch)], cl[:, r, :], start=True, stop=True)
                            if ch == CH or not last:
                                ins = nc.tensor.matmul(A[1][:, pr], kw_sb[:, b, i, :], mv[:, ch, hd, :], start=True, stop=True)
                        ins.then_inc(ml_b, 1)
                elif step[0] == "hm" and step[1] == 1:
                    c = step[2]
                    pe.wait_ge(hm_nrm, c + 1)
                    if c >= 4:
                        pe.wait_ge(hm_out, c - 3)
                    for hd in range(MH):
                        ins = nc.tensor.transpose(A[c % 4][:, hd * P:(hd + 1) * P], hsum[:, c, hd * 128:(hd + 1) * 128],
                                                  ident)
                    ins.then_inc(hm_tr, 1)
                elif step[0] == "out_start":
                    pe.wait_ge(hm_out, TT)
                elif step[0] == "turn2":
                    t = step[1]
                    pe.wait_ge(xn_rd, t + 1)
                    for hh in range(2):
                        m = 2 * t + hh
                        if m >= 3:
                            pe.wait_ge(n2_ev, m - 2)
                        for kk in range(4):
                            ins = nc.tensor.transpose(ps[:, 2 + m % 3, kk * P:(kk + 1) * P],
                                                      xn[:, t % 2, tok(4 * hh + kk)], ident)
                        ins.then_inc(n2_tr, 1)


def constants():
    import numpy as np
    c = np.zeros((P, 736), np.float32)
    c[:, 0:128] = np.eye(P)
    s, t = np.arange(P)[:, None], np.arange(P)[None, :]
    c[:, 128:256] = np.where(s > t, BIG, 0)
    c[:, 256:384] = np.where(s < t, BIG, 0)
    for y, j in enumerate((0, 1, 3)):
        q = j * QB + QB - 1 - np.arange(P)[:, None] % QB
        k = KSTART[j] + np.arange(KB)[None, :]
        lo = np.clip(q - KW // 2, 0, GRID - KW)
        c[:, 384 + y * KB:384 + (y + 1) * KB] = np.where((k >= lo) & (k < lo + KW), 0, -BIG)
    for v in range(2):
        c[v, 480 + v * P:480 + (v + 1) * P] = 1
        c[v + 2, 480 + v * P:480 + (v + 1) * P] = 1
    return c


_WEIGHTS = ["w_ada", "w_in", "w_br_na", "w_br_m", "w_br_cv", "w_out", "w_ffn_gate", "w_ffn_up", "w_ffn_down"]
_PLAIN = ["x_prompt", "x_sample", "cache_k", "cache_v", "state_C", "state_n", "b_ada", "g_post_mix", "g_post_ffn"]
_OUTS = dict(yp=(1, CTX, D), ys=(1, LAT, D), k=(1, 1, HEADS, CTX, DH), v=(1, 1, HEADS, CTX, DH),
             C=(1, 1, 2, MH, DK, 128), n=(1, 1, 2, MH, DK), m=(1, 1, 2, MH))


def kernel(**inputs):
    import numpy as np
    import concourse.bacc as bacc
    from concourse.bass_utils import run_bass_kernel_spmd

    x = {n: np.ascontiguousarray(v) for n, v in inputs.items()}
    given = {n: x[n] for n in _WEIGHTS + _PLAIN}
    given["consts"] = constants()
    given["rows"] = np.concatenate([x[n].reshape(-1, P) for n in (
        "b_ada", "g_pre_mix", "g_pre_ffn", "b_gate", "m_norm_g", "conv_w", "c", "c_ctx")])
    rpb = np.zeros((HEADS, 16, 64), x["na_rpb"].dtype)
    rpb[:, 0:15, 16:47] = x["na_rpb"][0]
    given["rpb"] = rpb
    gb = np.zeros((RW, 3), x["m_b_i"].dtype)
    for d in range(2):
        gb[32 * d:32 * d + MH, 0] = x["m_b_i"][0, d]
        gb[32 * d:32 * d + MH, 1] = x["m_b_f"][0, d]
        gb[32 * d:32 * d + MH, 2] = x["state_m"][0, 0, d]
    given["gbias"] = gb

    nc = bacc.Bacc("TRN2", target_bir_lowering=False, num_devices=1)
    a = {n: nc.dram_tensor("in_" + n, v.shape, F32, kind="ExternalInput").ap() for n, v in given.items()}
    out = {n: nc.dram_tensor("out_" + n, shape, F32, kind="ExternalOutput").ap() for n, shape in _OUTS.items()}
    program(nc, a, out)
    r = run_bass_kernel_spmd(nc, [{"in_" + n: v for n, v in given.items()}], core_ids=[0])
    return tuple(r.results[0]["out_" + n] for n in _OUTS)
```

```python
import concourse.bass as bass
from concourse import mybir
from contextlib import ExitStack

F32 = mybir.dt.float32
F32R = mybir.dt.float32r
ALU = mybir.AluOpType
ACT = mybir.ActivationFunctionType
X = mybir.AxisListType.X

P = 128
D = 1024
KD = D // P
CTX, LAT = 128, 512
T = LAT + CTX
HT = T // 2
TT = T // P
EPS = 1e-6
HEADS, DH = 8, 64
GRID, ROWS = 64, LAT // 64
QB, KB, KW = 16, 32, 16
NQB = GRID // QB
KSTART = [min(max(j * QB - KW // 2, 0), GRID - KB) for j in range(NQB)]
SHIFT = [16 - (j * QB - KSTART[j]) for j in range(NQB)]
BTYPE = [0, 1, 1, 2]
NKEY = ROWS * KB + CTX
MH, DK = 4, 128
CH = LAT // P
RW = 36
FF = 2816
FK = FF // P
UW = 256
BIG = 1e30
ROOM = 212832
NA_SCALE = DH ** -0.5
M_SCALE = DK ** -0.5

C_NAQ, C_NAK, C_NAV, C_MQ, C_MK, C_MV, C_MO, C_MIF = 0, 512, 1024, 1536, 2048, 2560, 3072, 3584
C_CB, C_CC, C_CX, C_GATE = 3600, 4112, 4624, 5136
R_BADA, R_GPM, R_GPF, R_BG, R_MG, R_CW, R_C = 0, 48, 56, 64, 88, 92, 104
NROWS = 120


DOWN_TILES = [2] + [4] * ((FK - 2) // 4)
DOWN_FIRST = [sum(DOWN_TILES[:i]) for i in range(len(DOWN_TILES))]


def weight_units():
    u = []
    ada = lambda which, i: ("ada", (which, i), KD, UW)
    for i in range(4):
        u += [ada(1, i), ada(0, i)]
    for p in range(2):
        u += [("q", p, KD, UW), ("k", p, KD, UW), ("v", p, KD, UW)]
    for kind in ("mq", "mk", "mv"):
        for p in range(2):
            u.append((kind, p, KD, UW))
    u.append(("mif", 0, KD, P))
    for p in range(2):
        u += [("cc", p, KD, UW), ("cx", p, KD, UW), ("cb", p, KD, UW)]
    late = {2: [[(4, i)] for i in range(4)], 0: [[(3, i)] for i in range(4)],
            1: [[(2, i), (5, i)] for i in range(4)]}
    for b in (2, 0, 1):
        if b == 0:
            u += [("mo", 0, KD, UW), ("mo", 1, KD, UW)]
        for i in range(4):
            u.append(("gate", (b, i), KD, UW))
            extra = [ada(*x) for x in late[b][i]]
            u += extra[:1]
            u.append(("br", (b, i), 4, UW))
            u += extra[1:]
    for r in range(2):
        for c in range(2):
            for h in range(2):
                u.append(("out", (c, h, r), 4, 512))
    for i in range(FK // 2):
        u += [("fg", i, KD, UW), ("fu", i, KD, UW)]
    for c in range(2):
        for i in range(6):
            u.append(("down", (c, i), DOWN_TILES[i], 512))
    return u


ROUND = [0, 0, 0, 1, 1]
UNITS = weight_units()
BLOCKS_HELD = 4


def parts_of(n):
    kind, _, kc, w = UNITS[n]
    return 1 if kind == "mif" else kc * w // 1024


BLOCKS = [(n, p) for n in range(len(UNITS)) for p in range(parts_of(n))]
BLOCK_OF = {np_: b for b, np_ in enumerate(BLOCKS)}


def block_shape(b):
    kind, _, kc, w = UNITS[BLOCKS[b][0]]
    if kind in ("ada", "br"):
        return 4, UW
    if kind in ("out", "down"):
        return 2, 512
    return KD, P


UNIT_OF = {(k, w): n for n, (k, w, _, _) in enumerate(UNITS)}
NA_UNITS = ([("lat", hp, j) for hp in (0, 1) for j in range(NQB)] + [("ctx", 0, 0)]
            + [("lat", hp, j) for hp in (2, 3) for j in range(NQB)] + [("ctx", 1, 0)])
ML_UNITS = []
for dr in range(2):
    for hp in range(2):
        ML_UNITS.append((CH, dr, hp, True, True))
for st in range(CH):
    for dr in range(2):
        for hp in range(2):
            ML_UNITS.append((st if dr == 0 else CH - 1 - st, dr, hp, st == 0, st == CH - 1))


def drain_engine(kind, what):
    return "V" if kind in ("cx", "cb", "br", "mif", "vt", "mvt", "ada_col", "fu", "kout", "out", "down") else "A"


FIRST_DOWN = ([0, 1], [2, 3, 4])


def make_plan():
    plan, groups = [], []

    def group(kind, unit, *what, bank=None):
        g = len(groups)
        groups.append(dict(kind=kind, unit=unit, what=what, eng=drain_engine(kind, what),
                           bank=g % 4 if bank is None else bank))
        plan.append(("group", g))
        return g

    def tiles(n):
        kind = UNITS[n][0]
        for f in range(2 if kind != "mif" else 1):
            for h in range(2):
                yield lambda f=f, h=h: group(kind, n, f, h)

    ahead = [0]

    def use(n, *parts):
        split_to(BLOCK_OF[n, parts[0]] + BLOCKS_HELD)
        for p in parts:
            plan.append(("use", BLOCK_OF[n, p]))

    def split_to(end):
        while ahead[0] < min(end, len(BLOCKS)):
            if UNITS[BLOCKS[ahead[0]][0]][0] == "mif":
                plan.append(("zero", ahead[0]))
            plan.append(("split", ahead[0]))
            ahead[0] += 1

    held = []
    side = []

    def unit(n):
        for j, emit in enumerate(tiles(n)):
            if j % 2 == 0 and j // 2 < parts_of(n):
                use(n, j // 2)
            if UNITS[n][:2] == ("br", (1, 3)) and j == 0:
                plan.append(("out_split", 0, 6))
            if UNITS[n][:2] == ("cc", 0) and j == 0:
                plan.append(("mstat",))
            if UNITS[n][:2] == ("cx", 0) and j == 0:
                plan.append(("mexp",))
            if UNITS[n][:2] == ("cx", 0) and j == 3:
                plan.append(("mcols",))
            if side:
                plan.extend(side.pop(0))
            if held:
                plan.append(held.pop())
            emit()
            x = groups[-1]
            if x["kind"] == "cx" and x["what"][1] == 1:
                held.append(("conv", UNITS[n][1], x["what"][0]))
            kind, turn = x["kind"], {"v": ("vt", 3), "mv": ("mvt", 2)}.get(x["kind"])
            if turn and x["what"] in ((1, 0), (1, 1)):
                for c in range(turn[1]):
                    group(turn[0], n, x["what"][1], c)

    split_to(2)
    plan.append(("xnorm",))
    for n in range(8):
        use(n, 0, 1)
        group("ada_row", n)
        if n < 4:
            plan.extend([("xturn", 2 * n), ("xturn", 2 * n + 1)])
        if n:
            group("ada_col", n - 1)
        if n in (2, 4, 6):
            plan.append(("h", n // 2 - 1))
        if n in (3, 5, 7):
            plan.append(("hsplit", n // 2 - 1))
    group("ada_col", 7)
    plan += [("h", 3), ("hsplit", 3)]
    plan.append(("kc",))
    plan.append(("bias0",))
    n = 8
    pending = []
    while UNITS[n][0] != "out":
        kind, which = UNITS[n][0], UNITS[n][1]
        if kind == "ada":
            use(n, 0, 1)
            group("ada_row", n)
            pending.append(n)
        else:
            if kind == "mif":
                for s in side:
                    plan.extend(s)
                side = []
                group("kout", n)
                plan.append(("na_end",))
            unit(n)
            while pending:
                group("ada_col", pending.pop(0))
        if kind == "v":
            if which == 0:
                N = len(NA_UNITS)
                for s in range(N + 2):
                    side += [[("na", 0, s)], [("na", 1, s)]]
        if kind == "cx" and which == 0:
            for s in range(len(ML_UNITS)):
                side += [[("ml", 0, s)], [("ml", 1, s)]]
        if kind == "mo" and which == 0:
            assert not side
            for c in range(TT):
                side.append([("hm", 0, c)])
        if kind == "mo" and which == 1:
            for c in range(TT + 2):
                side.append([("hm", 1, c)] * (c < TT) + [("hm", 2, c - 2)] * (c >= 2))
        n += 1
    while pending:
        group("ada_col", pending.pop(0))
    plan += [("out_split", 6, 8), ("out_start",)]
    slots = {}
    for t, times in enumerate(((0, 1, 2, 3, 5), (2, 3, 4, 5, 7), (4, 5, 6, 7, 9), (9, 10, 10, 11, 12),
                               (10, 11, 12, 13, 14))):
        for time, stage in zip(times, ("resid", "square2", "scale2", "turn2", "split2")):
            slots.setdefault(time, []).append((stage, t))

    def out_unit(c, h, r, banks):
        m = UNIT_OF[("out", (c, h, r))]
        use(m, 0, 1)
        for t in range(TT):
            if ROUND[t] == r:
                if h:
                    group("out", m, c, t, bank=banks[t])
                else:
                    plan.append(("part", "out", c, t, 0))
                yield

    slot = 0
    for r, banks in ((0, ((0, 1, 2), (3, 4, 5))), (1, ((None, None, None, 0, 1), (None, None, None, 6, 7)))):
        for c in range(2):
            for h in range(2):
                for _ in out_unit(c, h, r, banks[c]):
                    if r or (c and h):
                        plan += slots.get(slot, [])
                        slot += 1

    def ff_group(k, i, f, h):
        group(k, UNIT_OF[(k, i)], f, h, bank=(4 if k == "fu" else 0) + 2 * h + f)

    for k in ("fg", "fu"):
        for p in range(2):
            if p == 0 and k == "fg":
                use(UNIT_OF[(k, 0)], 0, 1)
            if p == 0 and k == "fu":
                plan += [("use", BLOCK_OF[UNIT_OF[(k, 0)], q]) for q in range(2)]
            ff_group(k, 0, p, 0)
            plan += slots.get(slot, [])
            slot += 1
    for k in ("fg", "fu"):
        for f in range(2):
            ff_group(k, 0, f, 1)
        if k == "fg":
            split_to(BLOCK_OF[UNIT_OF[("fg", 1)], 0] + 2)
    split_to(BLOCK_OF[UNIT_OF[("fg", 1)], 0] + BLOCKS_HELD - 1)
    rounds = []
    for i in range(1, FK // 2):
        rounds.append(len(plan))
        for k in ("fg", "fu"):
            m = UNIT_OF[(k, i)]
            last = (k, i) == ("fu", FK // 2 - 1)
            if last:
                use(m, 0, 1)
            for f, h in [(0, 0), (1, 0), (0, 1), (1, 1)] if last else [(0, 0), (0, 1), (1, 0), (1, 1)]:
                if h == 0 and not last:
                    use(m, f)
                ff_group(k, i, f, h)
                if f == 1 and last:
                    for piece in FIRST_DOWN[h]:
                        plan.append(("down_start", piece))
    for c in range(2):
        for i in range(6):
            m = UNIT_OF[("down", (c, i))]
            plan.append(("down_unit", 6 * c + i))
            use(m, *range(parts_of(m)))
            for t in range(TT):
                if i == 5:
                    group("down", m, c, t, bank=(5 * c + t) % 8)
                    if c == 1 and t:
                        plan.append(("final", t - 1))
                    if c == 1 and t == TT - 1:
                        plan.append(("final", t))
                else:
                    plan.append(("part", "down", c, t, i))
    return plan, groups, rounds


PLAN, GROUPS, _rounds = make_plan()
FF_FIRST, FF_ROUNDS = 2, FK // 2 - 4
FF_BODY = PLAN[_rounds[FF_FIRST - 1]:_rounds[FF_FIRST]]
PROGRAM = PLAN[:_rounds[FF_FIRST - 1]] + [("ff_loop",)] + PLAN[_rounds[FF_FIRST - 1 + FF_ROUNDS]:]
GROUPS_A_ROUND = 8
DRAINS_A_ROUND = 4
assert BLOCKS_HELD == 4


def drains(eng, g):
    return sum(1 for x in GROUPS[:g + 1] if x["eng"] == eng)


def last_user(bank, g):
    prev = [i for i in range(g) if GROUPS[i]["bank"] == bank]
    return prev[-1] if prev else None


def release_of(b):
    n, p = BLOCKS[b]
    by_column = block_shape(b) == (KD, P)
    mine = [g for g, x in enumerate(GROUPS) if x["unit"] == n and x["kind"] not in ("ada_col", "vt", "mvt", "kout")
            and (not by_column or x["what"][0] == p)]
    if mine:
        return "gemm", max(mine) + 1
    kind, which = UNITS[n][:2]
    parts = [s for s in PLAN if s[0] == "part"]
    return "part", 1 + max(i for i, (_, k, c, t, j) in enumerate(parts)
                           if k == kind and (c, j) == which[:2] and which[2:] in ((), (ROUND[t],)))


def lo_engine(b):
    return "V" if BLOCKS[b][0] <= UNIT_OF[("mif", 0)] else "P"


def lo_ready(b):
    e = lo_engine(b)
    return e, sum(1 for i in range(b + 1) if lo_engine(i) == e)


ADA = [n for n, u in enumerate(UNITS) if u[0] == "ada"]


def ada_slot(n):
    return ADA.index(n) % 2


RELEASE = [release_of(b) for b in range(len(BLOCKS))]
LAST = {}
for _g, _x in enumerate(GROUPS):
    LAST[(_x["kind"], UNITS[_x["unit"]][1] if _x["kind"] not in ("kout",) else 0, _x["what"])] = _g


def gid(kind, which, *what):
    return LAST[(kind, which, what)]


def program(nc, a, out):
    ctx = ExitStack()
    with ctx:
        base = (nc.sbuf_base + 31) // 32 * 32
        ctx.enter_context(nc.sbuf_tensor("whole", [P, ROOM // 4], F32))

        def at(name, shape, offset, dt=F32):
            size = 4
            for n in shape[1:]:
                size *= n
            assert offset + size <= ROOM, name
            return nc.alloc_sbuf_tensor_at(name, shape, dt, offset=base + offset)

        def chain(start, *items):
            got = []
            for name, shape, dt in items:
                got.append(at(name, shape, start, dt))
                size = 4
                for n in shape[1:]:
                    size *= n
                start += (size + 31) // 32 * 32
            return got, start

        (raw, w_hi, w_lo, h_hi, h_lo), R0 = chain(
            0, ("raw", [P, BLOCKS_HELD, 1024], F32), ("w_hi", [P, BLOCKS_HELD, 1024], F32R),
            ("w_lo", [P, BLOCKS_HELD, 1024], F32R),
            ("h_hi", [P, KD, T], F32R), ("h_lo", [P, KD, T], F32R))
        (cst, cols, mod, half_bg, cond, sil, small, adarow, gbias, neghalf), R1 = chain(
            R0, ("cst", [P, 736], F32), ("cols", [P, NROWS], F32), ("mod", [P, 4, KD, 2], F32),
            ("half_bg", [P, 24], F32), ("cond", [P, KD, 4], F32R), ("sil", [P, 16], F32),
            ("small", [P, 64], F32), ("adarow", [4, 2, UW], F32), ("gbias", [RW, 3], F32),
            ("neghalf", [P, 8], F32))
        ident = cst[:, 0:128]
        mask_m = cst[:, 128:384].rearrange("p (d t) -> p d t", d=2)
        mask_na = cst[:, 384:480].rearrange("p (y k) -> p y k", y=3)
        sel = cst[0:4, 480:736].rearrange("p (c m) -> p c m", c=2)
        (naq, nak, vtok, kct, vg, bm, braw, sx, pt), _e = chain(
            R1, ("naq", [P, 4, T], F32), ("nak", [P, 4, T], F32), ("vtok", [P, 10, 512], F32),
            ("kct", [P, 4, CTX], F32), ("vg", [P, 9, P], F32), ("bm", [P, 3, 2, NKEY], F32),
            ("braw", [P, 2, 512], F32), ("sx", [P, 2, 2, NKEY], F32), ("pt", [P, 2, 2, NKEY], F32))
        MQ = ROOM - 10240 * 3 - 10336
        assert _e <= MQ, _e
        (mq, mk, mv, att), _ = chain(
            MQ, ("mq", [P, MH, T], F32), ("mk", [P, MH, T], F32), ("mv", [P, TT, MH, 129], F32),
            ("att", [P, 4, T], F32))
        xt = at("xt", [P, TT, D], R1)
        xnt = at("xnt", [P, KD, T], R1 + 20480)
        rows = at("rows", [NROWS, P], R1 + 61440)
        kcr = at("kcr", [P, 512], R1 + 62464)
        junk = at("junk", [P, D], MQ)
        (bo_hi, bo_lo, cl, cout, hsum, mnat, mcols, dec, e_sb, st_sb, kw_sb, tmp_sb, num_sb, merged, gt), _e = chain(
            R1, ("bo_hi", [P, 4, T], F32R), ("bo_lo", [P, 4, T], F32R), ("cl", [P, 8, 129], F32),
            ("cout", [P, 2, 2, 129], F32), ("hsum", [P, TT, 512], F32), ("mnat", [RW, T], F32),
            ("mcols", [P, TT, 4, 8], F32), ("dec", [P, 8, CH], F32), ("e_sb", [P, 2, 2, P], F32),
            ("st_sb", [P, 2, 2, P], F32), ("kw_sb", [P, 2, 2, P], F32), ("tmp_sb", [P, 2, 129], F32),
            ("num_sb", [P, 2, 129], F32), ("merged", [P, KD, T], F32), ("gt", [P, 2, T], F32))
        assert _e <= MQ, (_e, MQ)
        MG = _e - 5120 - 20480
        cu = at("cu", [P, 2, T], MG)
        t1 = at("t1", [P, 2, T], MG + 5120)
        ib = at("ib", [RW, T], R1 + 20480 * 2 + 2048)
        lf = at("lf", [RW, T], R1 + 20480 * 2 + 2048 + 2560)
        st = [at(f"stat{i}", [RW, T], R1 + 2560 * i) for i in range(7)]
        mo = at("mo", [P, MH, T], MQ)
        hmt = at("hmt", [P, MH, T], MQ + 10240)
        g1 = at("g1", [P, 2, D], MQ + 20480)
        bb1 = at("bb1", [P, 2, D], MQ + 20480 + 10336)
        g2 = at("g2", [P, 2, D], R1 + 20480)
        bb2 = at("bb2", [P, 2, D], R1 + 20480 + 8192)
        x1 = at("x1", [P, TT, D], R1)
        (xb, xn, junk2), _e = chain(
            R1 + 20480 + 8192 + 27648, ("xb", [P, 2, D], F32), ("xn", [P, 2, D], F32), ("junk2", [P, D], F32))
        h32 = at("h32", [P, 2, KD, P], _e)
        (ff, sg, y2, yb, yb_junk), _e = chain(
            R1 + 20480 + 8192, ("ff", [P, FK, T], F32), ("sg", [P, 4, HT], F32),
            ("y2", [P, TT, 512], F32), ("yb", [P, 2, 512], F32), ("yb_junk", [P, 512], F32))
        assert _e <= ROOM
        ps = ctx.enter_context(nc.psum_tensor("ps", [P, 8, 512], F32))
        A = [ps[:, 4 + i, :] for i in range(4)]

        def sem(name):
            return ctx.enter_context(nc.semaphore(name))

        def sems(names):
            return [sem(n) for n in names.split()]

        const_in, rows_in, kc_in, gb_in = sems("const_in rows_in kc_in gb_in")
        x_in = [sem(f"x_in{t}") for t in range(TT)]
        raw_in = [sem(f"raw_in{i}") for i in range(BLOCKS_HELD)]
        vc_in, br0_in, br_in, state_in = sems("vc_in br0_in br_in state_in")
        bc1_in, bc2_in = sems("bc1_in bc2_in")
        xb_in = sems("xb_in0 xb_in1")
        hi_done, lo_by = sem("hi_done"), dict(V=sem("lo_by_vector"), P=sem("lo_by_pool"))
        mif_zero = sem("mif_zero")
        gemm_done, part_done, act_drain, dve_drain = sems("gemm_done part_done act_drain dve_drain")
        act_order, dve_order, pool_order = sems("act_order dve_order pool_order")
        cols_tr, cols_rd, cond_hi, cond_rd, kc_tr, kc_rd = sems("cols_tr cols_rd cond_hi cond_rd kc_tr kc_rd")
        x_sq, x_rstd, x_nrm, xl_tr, xc_tr = sems("x_sq x_rstd x_nrm xl_tr xc_tr")
        xt_dve, xt_act, xc_dve = sems("xt_dve xt_act xc_dve")
        mod_in, h_aff, h_hid, h_lod = sems("mod_in h_aff h_hid h_lod")
        bias_rd, bias_zero, mv_ones = sems("bias_rd bias_zero mv_ones")
        na_sc, na_add, na_max, na_exp, na_prob, na_tr, na_pt, na_pv, na_out = sems(
            "na_sc na_add na_max na_exp na_prob na_tr na_pt na_pv na_out")
        f_neg, f_exp, f_ln, s_exp_in, s_exp, nat_rd, ms_tr, ms_rd, m_fin = sems(
            "f_neg f_exp f_ln s_exp_in s_exp nat_rd ms_tr ms_rd m_fin")
        ml_a, ml_dm, ml_e, ml_kw, ml_st, ml_b, ml_tmp, ml_c, ml_h = sems(
            "ml_a ml_dm ml_e ml_kw ml_st ml_b ml_tmp ml_c ml_h")
        conv_rd, bo_hid, bo_lod, merged_add = sems("conv_rd bo_hid bo_lod merged_add")
        mo_rd, hm_sq, hm_rstd, hm_nrm, hm_tr, hm_out = sems("mo_rd hm_sq hm_rstd hm_nrm hm_tr hm_out")
        mg_hid, mg_lod, y0_sq, y_sq, y_rstd, x1_rd = sems("mg_hid mg_lod y0_sq y_sq y_rstd x1_rd")
        x1_sq, x1_rstd, xn_rd, n2_tr, n2_ev, n2_hid, n2_lod = sems("x1_sq x1_rstd xn_rd n2_tr n2_ev n2_hid n2_lod")
        ffs_hi, ffs_lo, z0_sq, z_sq, z_rstd, fin_rd = sems("ffs_hi ffs_lo z0_sq z_sq z_rstd fin_rd")
        stored, c_out = sem("stored"), sems("c_out0 c_out1")
        block = ctx.enter_context(nc.Block())

        def half(h):
            return slice(h * HT, (h + 1) * HT)

        def tok(t):
            return slice(t * P, (t + 1) * P)

        def wait_release(eng, b, rnd=0):
            kind, value = RELEASE[b]
            eng.wait_ge(gemm_done if kind == "gemm" else part_done, value + GROUPS_A_ROUND * rnd)

        def wait_lo(eng, b, rnd=0):
            e, value = lo_ready(b)
            eng.wait_ge(lo_by[e], value + BLOCKS_HELD * rnd)

        def block_of(buf, b):
            kc, w = block_shape(b)
            return buf[:, b % BLOCKS_HELD, :].rearrange("p (k w) -> p k w", k=kc)

        def raw_mif(b):
            return raw[:, b % BLOCKS_HELD, 0:KD * 16]

        def split_low(ve, eng, b, rnd=0):
            eng.wait_ge(hi_done, b + 1 + BLOCKS_HELD * rnd)
            s = b % BLOCKS_HELD
            if UNITS[BLOCKS[b][0]][0] == "mif":
                v = lambda buf: block_of(buf, b).rearrange("p k (g c) -> p k g c", g=4)[:, :, :, 0:4]
                r = raw_mif(b).rearrange("p (k g c) -> p k g c", k=KD, g=4)
                for k in range(KD):
                    ins = ve.tensor_tensor(v(w_lo)[:, k], r[:, k], v(w_hi).bitcast(F32)[:, k], ALU.subtract)
            else:
                ins = ve.tensor_tensor(w_lo[:, s, :], raw[:, s, :], w_hi[:, s, :].bitcast(F32), ALU.subtract)
            ins.then_inc(lo_by[lo_engine(b)], 1)

        def weight(buf, n, k, f=0):
            kind = UNITS[n][0]
            if kind == "br":
                return block_of(buf, BLOCK_OF[n, 0])[:, k, f * P:(f + 1) * P]
            if kind in ("ada", "out", "down"):
                per = block_shape(BLOCK_OF[n, 0])[0]
                return block_of(buf, BLOCK_OF[n, k // per])[:, k % per, :]
            return block_of(buf, BLOCK_OF[n, f])[:, k, :]

        def source(b, rnd=0):
            n, part = BLOCKS[b]
            kind, which = UNITS[n][:2]
            kc, w = block_shape(b)
            k0, c0 = 0, 0
            if kind == "ada":
                m, k0, c0 = "w_ada", 4 * part, which[0] * D + which[1] * UW
            elif kind == "br":
                m, c0 = ("w_br_na", "w_br_m", "w_br_cv")[which[0]], which[1] * UW
            elif kind == "out":
                m, k0, c0 = "w_out", 4 * which[1] + 2 * part, which[0] * 512
            elif kind == "down":
                m, k0, c0 = "w_ffn_down", DOWN_FIRST[which[1]] + 2 * part, which[0] * 512
            elif kind in ("fg", "fu"):
                m = "w_ffn_gate" if kind == "fg" else "w_ffn_up"
                return a[m][0, :, bass.ds(which * UW + part * P + rnd * UW, P)].rearrange("(k p) w -> p k w", p=P)
            elif kind == "gate":
                m, c0 = "w_in", C_GATE + which[0] * D + which[1] * UW + part * P
            elif kind == "mif":
                m, c0, w = "w_in", C_MIF, 16
            else:
                m = "w_in"
                c0 = dict(q=C_NAQ, k=C_NAK, v=C_NAV, mq=C_MQ, mk=C_MK, mv=C_MV, mo=C_MO, cc=C_CC, cx=C_CX,
                          cb=C_CB)[kind] + which * UW + part * P
            return a[m][0, k0 * P:(k0 + kc) * P, c0:c0 + w].rearrange("(k p) w -> p k w", p=P)

        def row_to_all(name, c0):
            return bass.AP(a[name].tensor, c0, [[0, P], [1, D]])

        def load_bias(eng, landed, hp):
            for i in range(2):
                for r in range(ROWS):
                    src = bass.AP(a["rpb"].tensor, (2 * hp + i) * 1024 + (7 - r) * 64, [[1, QB], [1, 512]])
                    eng.dma_start(braw[QB * r:QB * (r + 1), i, :], src).then_inc(landed, 16)

        @block.sync
        def _(sp):
            sp.dma_start(cst[:, :], a["consts"]).then_inc(const_in, 16)
            sp.dma_start(rows[:, :], a["rows"]).then_inc(rows_in, 16)
            def load(b, rnd=0):
                if b >= BLOCKS_HELD:
                    wait_lo(sp, b - BLOCKS_HELD, rnd)
                mif = UNITS[BLOCKS[b][0]][0] == "mif"
                dst = raw_mif(b).rearrange("p (k w) -> p k w", k=KD) if mif else block_of(raw, b)
                sp.dma_start(dst, source(b, rnd)).then_inc(raw_in[b % BLOCKS_HELD], 16)

            def load_x(t):
                if t >= 2:
                    sp.wait_ge(x1_rd, t - 1)
                src = a["x_sample"][0, tok(t), :] if t < CH else a["x_prompt"][0]
                sp.dma_start(xb[:, t % 2, :], src).then_inc(xb_in[t % 2], 16)

            load(0)
            load(1)
            for t in range(TT):
                src = a["x_sample"][0, tok(t), :] if t < CH else a["x_prompt"][0]
                sp.dma_start(xt[:, t, :], src).then_inc(x_in[t], 16)
            load(2)
            load(3)
            sp.dma_start(kcr[:, :].rearrange("p (h d) -> p h d", h=HEADS),
                         a["cache_k"][0, 0].rearrange("h p d -> p h d")).then_inc(kc_in, 16)
            for step in PROGRAM:
                if step[0] == "ff_loop":
                    with sp.Fori(0, FF_ROUNDS) as rnd:
                        for s in FF_BODY:
                            if s[0] == "split":
                                load(s[1] + BLOCKS_HELD, rnd)
                elif step[0] == "split":
                    if step[1] + BLOCKS_HELD < len(BLOCKS):
                        load(step[1] + BLOCKS_HELD)
                elif step[0] == "na_end":
                    g = gid("kout", 0)
                    sp.wait_ge(dve_drain, drains("V", g))
                    sp.dma_start(out["k"][0, 0].rearrange("h s d -> s h d"),
                                 sx[:, 0, :, :].rearrange("p a k -> p (a k)")[:, 0:512].rearrange(
                                     "p (h d) -> p h d", h=HEADS)).then_inc(stored, 16)
                    sp.dma_start(out["v"][0, 0].rearrange("h s d -> s h d"),
                                 vtok[:, 8, :].rearrange("p (h d) -> p h d", h=HEADS)).then_inc(stored, 16)
                elif step[0] == "kc":
                    load_bias(sp, br0_in, 0)
                elif step[0] == "ml" and step[1] == 1 and ML_UNITS[step[2]][0] == CH:
                    n = step[2]
                    _, dr, hp, _, _ = ML_UNITS[n]
                    sp.wait_ge(ml_c, n + 1)
                    sp.dma_start(out["C"][0, 0, dr, 2 * hp:2 * hp + 2].rearrange("h d e -> d h e"),
                                 cout[:, n % 2, :, 0:128]).then_inc(c_out[n % 2], 16)
                    sp.dma_start(out["n"][0, 0, dr, 2 * hp:2 * hp + 2].rearrange("h d -> d h"),
                                 cout[:, n % 2, :, 128], allow_slow_non_contiguous=True).then_inc(c_out[n % 2], 16)
                elif step[0] == "out_start":
                    sp.wait_ge(mg_lod, KD)
                    load_x(0)
                    load_x(1)
                elif step[0] == "resid" and step[1] + 2 < TT:
                    load_x(step[1] + 2)
                elif step[0] == "final":
                    t = step[1]
                    sp.wait_ge(fin_rd, t + 1)
                    dst = out["ys"][0, tok(t), :] if t < CH else out["yp"][0]
                    sp.dma_start(dst, x1[:, t, :]).then_inc(stored, 16)
            sp.wait_ge(m_fin, 1)
            sp.dma_start(out["m"][0, 0, 0, :].rearrange("(h o) -> h o", o=1), small[0:4, 40:41]).then_inc(stored, 16)
            sp.dma_start(out["m"][0, 0, 1, :].rearrange("(h o) -> h o", o=1), small[32:36, 40:41]).then_inc(stored, 16)
            for s in c_out:
                sp.wait_ge(s, 64)
            sp.wait_ge(stored, 16 * (2 + TT + 2))

        @block.gpsimd
        def _(pool):
            seen = [0]

            def link(ins):
                seen[0] += 1
                ins.then_inc(pool_order, 1)
                pool.wait_ge(pool_order, seen[0])

            def rstd(dst, src, width, n):
                link(nc.gpsimd.tensor_scalar(dst, src, 1.0 / n, EPS, ALU.mult, ALU.add))
                return nc.gpsimd.tensor_tensor(dst, dst, neghalf[:, 0:width], ALU.pow)

            link(nc.gpsimd.memset(neghalf[:, :], -0.5))
            nc.gpsimd.memset(bm[:, :, :, 256:NKEY], 0.0).then_inc(bias_zero, 1)
            nc.gpsimd.memset(mv[:, :, :, 128:129], 1.0).then_inc(mv_ones, 1)
            pool.dma_start(gbias[:, :], a["gbias"]).then_inc(gb_in, 16)
            for t in range(TT):
                pool.wait_ge(x_sq, t + 1)
                rstd(small[:, 8 + t:9 + t], small[:, t:t + 1], 1, D).then_inc(x_rstd, 1)

            def bias(hp):
                if hp == 0:
                    pool.wait_ge(br0_in, 16 * 2 * ROWS)
                else:
                    pool.wait_ge(br_in, 16 * 2 * ROWS * hp)
                first = [0, 4, 9, 13][hp]
                for y, free in ((0, 1), (1, 3), (2, 4)):
                    if hp:
                        pool.wait_ge(na_add, [0, 4, 9, 13][hp - 1] + free)
                    sh = (16, 8, 0)[y]
                    for i in range(2):
                        ins = nc.gpsimd.tensor_tensor(
                            bm[:, y, i, 0:256].rearrange("p (r k) -> p r k", r=ROWS),
                            braw[:, i, :].rearrange("p (r k) -> p r k", r=ROWS)[:, :, sh:sh + KB],
                            mask_na[:, y, :].unsqueeze(1).to_broadcast([P, ROWS, KB]), ALU.add)
                    ins.then_inc(bias_rd, 1)

            pool.wait_ge(const_in, 16)
            for step in PROGRAM:
                if step[0] == "ff_loop":
                    with pool.Fori(0, FF_ROUNDS) as rnd:
                        for s in FF_BODY:
                            if s[0] == "split":
                                split_low(nc.gpsimd, pool, s[1], rnd)
                elif step[0] == "split" and lo_engine(step[1]) == "P":
                    split_low(nc.gpsimd, pool, step[1])
                elif step[0] == "h":
                    i = step[1]
                    pool.wait_ge(xt_act, i + 1)
                    pool.wait_ge(xt_dve, i + 1)
                    pool.wait_ge(xc_dve, i // 2 + 1)
                    pool.wait_ge(mod_in, i + 1)
                    pool.wait_ge(dve_drain, drains("V", gid("ada_col", (0, i))))
                    for k in (2 * i, 2 * i + 1):
                        for c, sl in ((0, slice(0, LAT)), (1, slice(LAT, T))):
                            ins = nc.gpsimd.tensor_scalar(xnt[:, k, sl], xnt[:, k, sl], mod[:, 0, k, c:c + 1],
                                                          mod[:, 1, k, c:c + 1], ALU.mult, ALU.add)
                        ins.then_inc(h_aff, 1)
                elif step[0] == "bias0":
                    pool.wait_ge(h_lod, KD)
                    pool.dma_start(vtok[:, 9, :].rearrange("p (h d) -> p h d", h=HEADS),
                                   a["cache_v"][0, 0].rearrange("h p d -> p h d")).then_inc(vc_in, 16)
                    bias(0)
                    pool.wait_ge(bias_rd, 3)
                    load_bias(pool, br_in, 1)
                elif step[0] == "na" and step[1] == 1 and step[2] in (1, 5, 10):
                    hp = {1: 1, 5: 2, 10: 3}[step[2]]
                    bias(hp)
                    if hp < 3:
                        pool.wait_ge(bias_rd, 3 * (hp + 1))
                        load_bias(pool, br_in, hp + 1)
                elif step[0] == "zero":
                    wait_release(pool, step[1] - BLOCKS_HELD)
                    s = step[1] % BLOCKS_HELD
                    nc.gpsimd.memset(w_hi[:, s, :].bitcast(F32), 0.0).then_inc(mif_zero, 1)
                    nc.gpsimd.memset(w_lo[:, s, :].bitcast(F32), 0.0).then_inc(mif_zero, 1)
                elif step[0] == "mstat":
                    pool.wait_ge(stored, 32)
                    pool.wait_ge(na_out, len(NA_UNITS))
                    pool.dma_start(cl[:, :, 0:128],
                                   a["state_C"][0, 0].rearrange("a h d e -> d (a h) e")).then_inc(state_in, 16)
                    pool.dma_start(cl[:, :, 128], a["state_n"][0, 0].rearrange("a h d -> d (a h)"),
                                   allow_slow_non_contiguous=True).then_inc(state_in, 16)
                elif step == ("use", BLOCK_OF[UNIT_OF[("gate", (1, 0))], 0]):
                    pool.wait_ge(bo_lod, 8)
                    pool.dma_start(bb1[:, 0, :], row_to_all("b_ada", 2 * D)).then_inc(bc1_in, 16)
                    pool.dma_start(bb1[:, 1, :], row_to_all("g_post_mix", 0)).then_inc(bc1_in, 16)
                    pool.wait_ge(hm_tr, TT)
                    pool.dma_start(bb2[:, 0, :], row_to_all("b_ada", 5 * D)).then_inc(bc2_in, 16)
                    pool.dma_start(bb2[:, 1, :], row_to_all("g_post_ffn", 0)).then_inc(bc2_in, 16)
                elif step[0] == "group" and GROUPS[step[1]]["kind"] == "mo":
                    x = GROUPS[step[1]]
                    f, h = x["what"]
                    pool.wait_ge(act_drain, drains("A", step[1]))
                    v = mo[:, 2 * UNITS[x["unit"]][1] + f, half(h)]
                    nc.gpsimd.tensor_scalar(v, v, 0.5, 0.5, ALU.mult, ALU.add).then_inc(mo_rd, 1)
                elif step[0] == "hm" and step[1] == 0:
                    c = step[2]
                    pool.wait_ge(hm_sq, c + 1)
                    v = small[:, 16 + 4 * c:20 + 4 * c] if c < 4 else small[:, 32:36]
                    rstd(v, v, 4, 128).then_inc(hm_rstd, 1)
                elif step[0] == "resid":
                    t = step[1]
                    pool.wait_ge(y_sq, t + 1)
                    v = small[:, t:t + 1]
                    link(nc.gpsimd.tensor_tensor(v, small[:, 44 + t:45 + t], small[:, 49 + t:50 + t], ALU.add))
                    rstd(v, v, 1, D).then_inc(y_rstd, 1)
                elif step[0] == "square2":
                    t = step[1]
                    pool.wait_ge(x1_sq, t + 1)
                    v = small[:, 8 + t:9 + t]
                    rstd(v, v, 1, D).then_inc(x1_rstd, 1)
                elif step[0] == "final":
                    t = step[1]
                    pool.wait_ge(z_sq, t + 1)
                    v = small[:, 16 + t:17 + t]
                    link(nc.gpsimd.tensor_tensor(v, small[:, 24 + t:25 + t], small[:, 32 + t:33 + t], ALU.add))
                    rstd(v, v, 1, D).then_inc(z_rstd, 1)

        @block.scalar
        def _(act):
            seen = [0]

            def link(ins):
                seen[0] += 1
                ins.then_inc(act_order, 1)
                act.wait_ge(act_order, seen[0])

            def split_hi(b, rnd=0):
                s = b % BLOCKS_HELD
                act.wait_ge(raw_in[s], 16 * (b // BLOCKS_HELD + 1) + 16 * rnd)
                if b >= BLOCKS_HELD:
                    wait_release(act, b - BLOCKS_HELD, rnd)
                if UNITS[BLOCKS[b][0]][0] == "mif":
                    act.wait_ge(mif_zero, 2)
                    w = block_of(w_hi, b).rearrange("p k (g c) -> p k g c", g=4)[:, :, :, 0:4]
                    r = raw_mif(b).rearrange("p (k g c) -> p k g c", k=KD, g=4)
                    for k in range(KD):
                        ins = nc.scalar.activation(w[:, k], r[:, k], ACT.Copy)
                else:
                    ins = nc.scalar.activation(w_hi[:, s, :], raw[:, s, :], ACT.Copy)
                ins.then_inc(hi_done, 1)

            def branch_hi(src, last_group, ready, k0):
                act.wait_ge(gemm_done, last_group + 1)
                act.wait_ge(*ready)
                for k in range(4):
                    nc.scalar.activation(bo_hi[:, k, :], src[:, k, :], ACT.Copy).then_inc(bo_hid, 1)

            def first_ff_hi(t):
                act.wait_ge(gemm_done, gid("fu", FK // 2 - 1, 1, 0 if t in FIRST_DOWN[0] else 1) + 1)
                act.wait_ge(dve_drain, drains("V", gid("fu", 0, 1, 1)))
                n = DOWN_TILES[0]
                nc.scalar.activation(h_hi[:, 0:n, tok(t)], ff[:, 0:n, tok(t)], ACT.Copy).then_inc(ffs_hi, 1)

            def ff_hi(o):
                kc, k0 = DOWN_TILES[o % 6], DOWN_FIRST[o % 6]
                if o < 2:
                    act.wait_ge(gemm_done, gid("fu", FK // 2 - 1, 1, 1) + 1)
                else:
                    wait_release(act, BLOCK_OF[UNIT_OF[("down", divmod(o - 2, 6))], 0])
                act.wait_ge(dve_drain, drains("V", gid("fu", FK // 2 - 1, 1, 1)))
                o2 = 4 * (o % 2)
                for k, n in ((0, kc // 2), (kc // 2, kc - kc // 2)):
                    nc.scalar.activation(h_hi[:, o2 + k:o2 + k + n, :], ff[:, k0 + k:k0 + k + n, :],
                                         ACT.Copy).then_inc(ffs_hi, 1)

            def drain(g, rnd=0):
                x = GROUPS[g]
                kind, n = x["kind"], x["unit"]
                if x["eng"] != "A" and kind not in ("out", "down", "cb"):
                    return
                which = UNITS[n][1]
                bank = ps[:, x["bank"], 0:HT]
                if kind == "q":
                    f, h = x["what"]
                    act.wait_ge(gemm_done, g + 1)
                    r0, r1 = (0, 5) if h == 0 else (5, ROWS)
                    v = naq[:, 2 * which + f, 0:LAT].rearrange(
                        "p (j r c) -> p j r c", j=NQB, r=ROWS)[:, :, r0:r1, ::-1]
                    src = bank[:, 0:(r1 - r0) * GRID].rearrange("p (r j c) -> p j r c", j=NQB, c=QB)
                    ins = nc.scalar.activation(v, src, ACT.Copy, scale=NA_SCALE)
                    if h == 1:
                        ins = nc.scalar.activation(naq[:, 2 * which + f, LAT:T], bank[:, HT - P:HT], ACT.Copy,
                                                   scale=NA_SCALE)
                    ins.then_inc(act_drain, 1)
                elif kind == "v":
                    f, h = x["what"]
                    act.wait_ge(gemm_done, g + 1)
                    if f == 1:
                        act.wait_ge(gemm_done, gid("vt", which, 0, 2) + 1)
                    elif which == 1:
                        act.wait_ge(gemm_done, gid("vt", 0, 1, 2) + 1)
                    r0, r1 = (0, 5) if h == 0 else (5, ROWS)
                    flat = vg[:, 0:8, :].rearrange("p a b -> p (a b)")
                    for j in range(NQB):
                        ins = nc.scalar.activation(
                            flat[:, (j * ROWS + r0) * KB:(j * ROWS + r1) * KB].rearrange("p (r k) -> p r k", k=KB),
                            bank[:, 0:(r1 - r0) * GRID].rearrange("p (r c) -> p r c", c=GRID)[
                                :, :, KSTART[j]:KSTART[j] + KB], ACT.Copy)
                    if h == 1:
                        ins = nc.scalar.activation(vg[:, 8, :], bank[:, HT - P:HT], ACT.Copy)
                    ins.then_inc(act_drain, 1)
                elif kind in ("mq", "k", "mk"):
                    dst, sc = dict(mq=(mq, M_SCALE), k=(nak, 1.0), mk=(mk, 1.0))[kind]
                    f, h = x["what"]
                    act.wait_ge(gemm_done, g + 1)
                    nc.scalar.activation(dst[:, 2 * which + f, half(h)], bank, ACT.Copy, scale=sc).then_inc(act_drain, 1)
                elif kind == "mv":
                    f, h = x["what"]
                    act.wait_ge(gemm_done, g + 1)
                    if f == 1:
                        act.wait_ge(gemm_done, gid("mvt", which, 0, 1) + 1)
                    v = vg[:, 0:TT, :].rearrange("p a b -> p (a b)")
                    nc.scalar.activation(v[:, half(h)], bank, ACT.Copy).then_inc(act_drain, 1)
                elif kind == "cc":
                    f, h = x["what"]
                    act.wait_ge(gemm_done, g + 1)
                    act.wait_ge(conv_rd, 2 * which)
                    nc.scalar.activation(cu[:, f, half(h)], bank, ACT.Copy).then_inc(act_drain, 1)
                elif kind == "cb":
                    f, h = x["what"]
                    if h == 1:
                        act.wait_ge(dve_drain, drains("V", g))
                        act.wait_ge(ms_rd, 3)
                        nc.scalar.activation(bo_hi[:, 2 * which + f, :], t1[:, f, :], ACT.Copy).then_inc(bo_hid, 1)
                elif kind == "gate":
                    f, h = x["what"]
                    b, i = which
                    act.wait_ge(gemm_done, g + 1)
                    before = 4 * (4 * (2, 0, 1).index(b) + i)
                    if before:
                        act.wait_ge(merged_add, before)
                    t = 8 * b + 2 * i + f
                    nc.scalar.activation(gt[:, f, half(h)], bank, ACT.Tanh, scale=0.5,
                                         bias=half_bg[:, t:t + 1]).then_inc(act_drain, 1)
                elif kind == "mo":
                    f, h = x["what"]
                    act.wait_ge(gemm_done, g + 1)
                    act.wait_ge(ml_h, len(ML_UNITS))
                    nc.scalar.activation(mo[:, 2 * which + f, half(h)], bank, ACT.Tanh, scale=0.5).then_inc(act_drain, 1)
                elif kind == "ada_row":
                    act.wait_ge(gemm_done, g + 1)
                    nc.scalar.activation(adarow[:, ada_slot(n), :], ps[0:4, x["bank"], 0:UW], ACT.Copy).then_inc(act_drain, 1)
                elif kind == "fg":
                    f, h = x["what"]
                    act.wait_ge(gemm_done, g + 1 + GROUPS_A_ROUND * rnd)
                    if which:
                        act.wait_ge(dve_drain, drains("V", gid("fu", which - 1, f, h)) + DRAINS_A_ROUND * rnd)
                    nc.scalar.activation(sg[:, 2 * f + h, :], bank, ACT.Silu).then_inc(act_drain, 1)
                elif kind in ("out", "down"):
                    c, t = x["what"]
                    full = ps[:, x["bank"], :]
                    act.wait_ge(gemm_done, g + 1)
                    b0, b1 = (44, 49) if kind == "out" else (24, 32)
                    done = dict(out=(y0_sq, y_sq), down=(z0_sq, z_sq))[kind][c]
                    col = (b1 if c else b0) + t
                    jk = junk2 if kind == "out" else yb_junk
                    ins = nc.scalar.activation(jk[:, 0:512], full, ACT.Square, accum_out=small[:, col:col + 1])
                    ins.then_inc(done, 1)
                    act.wait_ge(done, t + 1)

            act.wait_ge(cols_rd, 1)
            link(nc.scalar.activation(sil[:, :], cols[:, R_C:R_C + 16], ACT.Silu))
            nc.scalar.activation(cond[:, :, 0:2], sil[:, :].rearrange("p (c k) -> p k c", c=2), ACT.Copy).then_inc(cond_hi, 1)
            for step in PROGRAM:
                if step[0] == "ff_loop":
                    with act.Fori(0, FF_ROUNDS) as rnd:
                        for s in FF_BODY:
                            if s[0] == "split":
                                split_hi(s[1], rnd)
                            elif s[0] == "group":
                                drain(s[1], rnd)
                elif step[0] == "split":
                    split_hi(step[1])
                elif step[0] == "xnorm":
                    for t in range(TT):
                        act.wait_ge(x_in[t], 16)
                        nc.scalar.activation(junk[:, :], xt[:, t, :], ACT.Square,
                                             accum_out=small[:, t:t + 1]).then_inc(x_sq, 1)
                        act.wait_ge(x_sq, t + 1)
                elif step[0] == "xturn" and step[1] % 2:
                    k = step[1]
                    act.wait_ge(xl_tr, k + 1)
                    nc.scalar.activation(xnt[:, k, 0:LAT], A[1], ACT.Copy).then_inc(xt_act, 1)
                elif step[0] == "down_unit":
                    if step[1] < 11:
                        ff_hi(step[1] + 1)
                elif step[0] == "use":
                    n, part = BLOCKS[step[1]]
                    if UNITS[n][:2] == ("gate", (0, 0)) and part == 0:
                        branch_hi(att, gid("br", (2, 3), 1, 1), (na_out, len(NA_UNITS)), 4)
                    if UNITS[n][:2] == ("gate", (1, 0)) and part == 0:
                        branch_hi(hmt, gid("br", (0, 3), 1, 1), (hm_out, TT), 8)
                elif step[0] == "group":
                    drain(step[1])
                elif step[0] == "hsplit":
                    for k in (2 * step[1], 2 * step[1] + 1):
                        act.wait_ge(h_aff, k + 1)
                        nc.scalar.activation(h_hi[:, k, :], xnt[:, k, :], ACT.Copy).then_inc(h_hid, 1)
                elif step[0] == "na":
                    _, sub, s = step
                    if sub == 0 and s < len(NA_UNITS):
                        lat = NA_UNITS[s][0] == "lat"
                        act.wait_ge(na_max, s + 1)
                        b = s % 2
                        m = 2 if lat else 4
                        w = NKEY if lat else CTX
                        for i in range(m):
                            v = sx[:, b, i, :] if lat else sx[:, b, i // 2, (i % 2) * CTX:(i % 2 + 1) * CTX]
                            ins = nc.scalar.activation(v, v, ACT.Exp, bias=small[:, 16 + i:17 + i],
                                                       accum_out=small[:, 20 + i:21 + i])
                        ins.then_inc(na_exp, 1)
                        act.wait_ge(na_exp, s + 1)
                    if sub == 1 and 0 <= s - 1 < len(NA_UNITS):
                        n = s - 1
                        w = NKEY if NA_UNITS[n][0] == "lat" else 2 * CTX
                        act.wait_ge(na_tr, n + 1)
                        if n >= 2:
                            act.wait_ge(na_pv, n - 1)
                        nc.scalar.activation(pt[:, n % 2, :, 0:w], ps[:, 6:8, 0:w], ACT.Copy).then_inc(na_pt, 1)
                elif step[0] == "mstat":
                    act.wait_ge(f_neg, 1)
                    nc.scalar.activation(st[1][:, :], st[0][:, :], ACT.Exp).then_inc(f_exp, 1)
                    act.wait_ge(f_exp, 1)
                    nc.scalar.activation(st[2][:, :], st[1][:, :], ACT.Ln, bias=1.0).then_inc(f_ln, 1)
                elif step[0] == "mexp":
                    act.wait_ge(s_exp_in, 1)
                    for i in (4, 5, 2):
                        ins = nc.scalar.activation(st[i][:, :], st[i][:, :], ACT.Exp)
                    ins.then_inc(s_exp, 1)
                elif step[0] == "ml":
                    _, sub, n = step
                    ch, dr, hp, first, last = ML_UNITS[n]
                    b = n % 2
                    if sub == 0:
                        act.wait_ge(ml_a, n + 1)
                        if n == 0:
                            act.wait_ge(ms_rd, 3)
                        for i in range(2):
                            r = dr * 4 + 2 * hp + i
                            ins = nc.scalar.activation(kw_sb[:, b, i, :], A[2][:, i * P:(i + 1) * P], ACT.Copy,
                                                       scale=mcols[:, ch, 2, r:r + 1])
                        ins.then_inc(ml_kw, 1)
                        act.wait_ge(ml_dm, n + 1)
                        nc.scalar.activation(e_sb[:, b], e_sb[:, b], ACT.Exp, scale=-1.0).then_inc(ml_e, 1)
                    elif ch < CH:
                        act.wait_ge(ml_b, n + 1)
                        for i in range(2):
                            r = dr * 4 + 2 * hp + i
                            ins = nc.scalar.activation(tmp_sb[:, i, :], A[0][:, i * 129:(i + 1) * 129], ACT.Copy,
                                                       scale=mcols[:, ch, 1, r:r + 1])
                        ins.then_inc(ml_tmp, 1)
                elif step[0] == "out_split":
                    _, k0, k1 = step
                    act.wait_ge(merged_add, 4 * (8 + k1 // 2))
                    act.wait_ge(gemm_done, gid("gate", (1, 3), 1, 1) + 1)
                    for k in range(k0, k1):
                        nc.scalar.activation(h_hi[:, k, :], merged[:, k, :], ACT.Copy, scale=0.5).then_inc(mg_hid, 1)
                elif step[0] == "down_start":
                    first_ff_hi(step[1])
                elif step[0] == "square2":
                    t = step[1]
                    act.wait_ge(x1_rd, t + 1)
                    nc.scalar.activation(junk2[:, :], x1[:, t, :], ACT.Square,
                                         accum_out=small[:, 8 + t:9 + t]).then_inc(x1_sq, 1)
                    act.wait_ge(x1_sq, t + 1)
                elif step[0] == "scale2":
                    t = step[1]
                    act.wait_ge(x1_rstd, t + 1)
                    if t >= 2:
                        act.wait_ge(n2_tr, 2 * t - 2)
                    nc.scalar.activation(xn[:, t % 2, :], x1[:, t, :], ACT.Copy,
                                         scale=small[:, 8 + t:9 + t]).then_inc(xn_rd, 1)
                elif step[0] == "split2":
                    t = step[1]
                    act.wait_ge(n2_ev, 2 * t + 2)
                    nc.scalar.activation(h_hi[:, :, tok(t)], h32[:, t % 2], ACT.Copy).then_inc(n2_hid, 1)

        @block.vector
        def _(dve):
            seen = [0]

            def link(ins):
                seen[0] += 1
                ins.then_inc(dve_order, 1)
                dve.wait_ge(dve_order, seen[0])

            def branch_lo(src, k0):
                for k in range(4):
                    dve.wait_ge(bo_hid, k0 + k + 1)
                    nc.vector.tensor_tensor(bo_lo[:, k, :], src[:, k, :], bo_hi[:, k, :].bitcast(F32),
                                            ALU.subtract).then_inc(bo_lod, 1)

            def ff_lo(o):
                kc, k0 = DOWN_TILES[o % 6], DOWN_FIRST[o % 6]
                o2 = 4 * (o % 2)
                for i, (k, n) in enumerate(((0, kc // 2), (kc // 2, kc - kc // 2))):
                    dve.wait_ge(ffs_hi, TT + 2 * o - 1 + i)
                    nc.vector.tensor_tensor(h_lo[:, o2 + k:o2 + k + n, :], ff[:, k0 + k:k0 + k + n, :],
                                            h_hi[:, o2 + k:o2 + k + n, :].bitcast(F32), ALU.subtract).then_inc(ffs_lo, 1)

            def drain(g, rnd=0):
                x = GROUPS[g]
                if x["eng"] != "V":
                    return
                kind, n = x["kind"], x["unit"]
                which = UNITS[n][1]
                full = ps[:, x["bank"], :]
                bank = full[:, 0:HT]
                if kind in ("out", "down"):
                    c, t = x["what"]
                    cnd = 0 if t < CH else 1
                    cc = slice(c * 512, (c + 1) * 512)
                    sq, gd = ((y0_sq, y_sq), g1) if kind == "out" else ((z0_sq, z_sq), g2)
                    dst = x1[:, t, cc] if kind == "out" else yb[:, t % 2, :] if c else y2[:, t, :]
                    dve.wait_ge(sq[c], t + 1)
                    nc.vector.tensor_tensor(dst, full, gd[:, cnd, cc], ALU.mult).then_inc(dve_drain, 1)
                    return
                dve.wait_ge(gemm_done, g + 1 + GROUPS_A_ROUND * rnd)
                if kind == "vt":
                    f, c = x["what"]
                    ft = 2 * which + f
                    if c < 2:
                        nc.vector.tensor_copy(vtok[:, 4 * c:4 * c + 4, tok(ft)],
                                              full.rearrange("p (a b) -> p a b", a=4)).then_inc(dve_drain, 1)
                    else:
                        nc.vector.tensor_copy(vtok[:, 8, tok(ft)], full[:, 0:P]).then_inc(dve_drain, 1)
                elif kind == "mvt":
                    f, c = x["what"]
                    ft = 2 * which + f
                    if c == 0:
                        nc.vector.tensor_copy(mv[:, 0:CH, ft, 0:128],
                                              full.rearrange("p (a b) -> p a b", a=4)).then_inc(dve_drain, 1)
                    else:
                        nc.vector.tensor_copy(mv[:, CH, ft, 0:128], full[:, 0:P]).then_inc(dve_drain, 1)
                elif kind == "kout":
                    nc.vector.tensor_copy(sx[:, 0, :, :].rearrange("p a k -> p (a k)")[:, 0:512], full).then_inc(dve_drain, 1)
                elif kind == "mif":
                    f, h = x["what"]
                    dve.wait_ge(gb_in, 16)
                    link(nc.vector.tensor_scalar(ib[:, half(h)], bank[0:RW], gbias[:, 0:1], None, ALU.add))
                    nc.vector.tensor_scalar(lf[:, half(h)], bank[64:64 + RW], gbias[:, 1:2], None,
                                            ALU.add).then_inc(dve_drain, 1)
                elif kind == "cx":
                    f, h = x["what"]
                    dve.wait_ge(act_drain, drains("A", gid("cc", which, f, h)))
                    v = cu[:, f, half(h)]
                    nc.vector.tensor_tensor(v, bank, v, ALU.mult).then_inc(dve_drain, 1)
                elif kind == "cb":
                    f, h = x["what"]
                    dve.wait_ge(conv_rd, 2 * which + f + 1)
                    v = t1[:, f, half(h)]
                    nc.vector.tensor_tensor(v, bank, v, ALU.mult).then_inc(dve_drain, 1)
                    if h == 1:
                        k = 2 * which + f
                        dve.wait_ge(bo_hid, k + 1)
                        nc.vector.tensor_tensor(bo_lo[:, k, :], t1[:, f, :], bo_hi[:, k, :].bitcast(F32),
                                                ALU.subtract).then_inc(bo_lod, 1)
                elif kind == "br":
                    f, h = x["what"]
                    b, i = which
                    dve.wait_ge(act_drain, drains("A", gid("gate", which, f, h)))
                    v = gt[:, f, half(h)]
                    mg = merged[:, 2 * i + f, half(h)]
                    nc.vector.scalar_tensor_tensor(v, v, 1.0, bank, ALU.add, ALU.mult).then_inc(dve_drain, 1)
                    dve.wait_ge(dve_drain, drains("V", g))
                    if b == 2:
                        nc.vector.tensor_copy(mg, v).then_inc(merged_add, 1)
                    else:
                        nc.vector.tensor_tensor(mg, mg, v, ALU.add).then_inc(merged_add, 1)
                elif kind == "ada_col":
                    m, i = which
                    if m in (2, 5):
                        gd, bb, landed = (g1, bb1, bc1_in) if m == 2 else (g2, bb2, bc2_in)
                        dve.wait_ge(landed, 32)
                        if m == 5:
                            for s in c_out:
                                dve.wait_ge(s, 64)
                        cc = slice(i * UW, (i + 1) * UW)
                        v = gd[:, :, cc]
                        nc.vector.tensor_tensor(v, full.rearrange("p (c w) -> p c w", c=2),
                                                bb[:, 0:1, cc].to_broadcast([P, 2, UW]), ALU.add).then_inc(dve_drain, 1)
                        dve.wait_ge(dve_drain, drains("V", g))
                        link(nc.vector.tensor_tensor(v, v, bb[:, 1:2, cc].to_broadcast([P, 2, UW]), ALU.mult))
                    else:
                        j = {1: 0, 0: 1, 4: 2, 3: 3}[m]
                        v = mod[:, j, 2 * i:2 * i + 2, :]
                        bc = cols[:, R_BADA + 8 * m + 2 * i:R_BADA + 8 * m + 2 * i + 2]
                        nc.vector.tensor_tensor(v, full[:, 0:4].rearrange("p (k c) -> p k c", k=2),
                                                bc.unsqueeze(2).to_broadcast([P, 2, 2]), ALU.add).then_inc(dve_drain, 1)
                        dve.wait_ge(dve_drain, drains("V", g))
                        if m in (1, 4):
                            r = (R_GPM if m == 1 else R_GPF) + 2 * i
                            nc.vector.scalar_tensor_tensor(
                                v, v, 1.0, cols[:, r:r + 2].unsqueeze(2).to_broadcast([P, 2, 2]),
                                ALU.add, ALU.mult).then_inc(mod_in, 1)
                elif kind == "fu":
                    f, h = x["what"]
                    dve.wait_ge(act_drain, drains("A", gid("fg", which, f, h)) + DRAINS_A_ROUND * rnd)
                    tile = ff[:, 2 * which + f, half(h)] if isinstance(rnd, int) else \
                        ff[:, :, :].rearrange("p k t -> p (k t)")[:, bass.ds((2 * which + f) * T + h * HT
                                                                             + rnd * (2 * T), HT)]
                    nc.vector.tensor_tensor(tile, bank, sg[:, 2 * f + h, :], ALU.mult).then_inc(dve_drain, 1)

            dve.wait_ge(cols_tr, 1)
            nc.vector.tensor_copy(cols[:, :], A[0][:, 0:NROWS]).then_inc(cols_rd, 1)
            dve.wait_ge(cols_rd, 1)
            link(nc.vector.tensor_scalar(half_bg[:, :], cols[:, R_BG:R_BG + 24], 0.5, None, ALU.mult))
            dve.wait_ge(cond_hi, 1)
            nc.vector.tensor_tensor(cond[:, :, 2:4], sil[:, :].rearrange("p (c k) -> p k c", c=2),
                                    cond[:, :, 0:2].bitcast(F32), ALU.subtract).then_inc(cond_rd, 1)
            written = set()
            for step in PROGRAM:
                if step[0] == "ff_loop":
                    with dve.Fori(0, FF_ROUNDS) as rnd:
                        for s in FF_BODY:
                            if s[0] == "group":
                                drain(s[1], rnd)
                elif step[0] == "split":
                    if lo_engine(step[1]) == "V":
                        split_low(nc.vector, dve, step[1])
                elif step[0] == "xnorm":
                    for t in range(TT):
                        dve.wait_ge(x_rstd, t + 1)
                        nc.vector.tensor_scalar(xt[:, t, :], xt[:, t, :], small[:, 8 + t:9 + t], None,
                                                ALU.mult).then_inc(x_nrm, 1)
                elif step[0] == "xturn":
                    k = step[1]
                    if k % 2 == 0:
                        dve.wait_ge(xl_tr, k + 1)
                        nc.vector.tensor_copy(xnt[:, k, 0:LAT], A[0]).then_inc(xt_dve, 1)
                    if k % 4 == 3:
                        i = k // 4
                        dve.wait_ge(xc_tr, i + 1)
                        nc.vector.tensor_copy(xnt[:, 4 * i:4 * i + 4, LAT:T],
                                              A[2 + i].rearrange("p (a b) -> p a b", a=4)).then_inc(xc_dve, 1)
                elif step[0] == "kc":
                    dve.wait_ge(kc_tr, 1)
                    nc.vector.tensor_copy(kct[:, :, :], A[1].rearrange("p (a b) -> p a b", a=4)).then_inc(kc_rd, 1)
                elif step[0] == "down_unit":
                    if step[1] < 11:
                        ff_lo(step[1] + 1)
                elif step[0] == "use":
                    n, part = BLOCKS[step[1]]
                    if UNITS[n][:2] == ("gate", (0, 0)) and part == 0:
                        branch_lo(att, 4)
                    if UNITS[n][:2] == ("gate", (1, 0)) and part == 0:
                        branch_lo(hmt, 8)
                elif step[0] == "group":
                    drain(step[1])
                elif step[0] == "hsplit":
                    for k in (2 * step[1], 2 * step[1] + 1):
                        dve.wait_ge(h_hid, k + 1)
                        nc.vector.tensor_tensor(h_lo[:, k, :], xnt[:, k, :], h_hi[:, k, :].bitcast(F32),
                                                ALU.subtract).then_inc(h_lod, 1)
                elif step[0] == "na":
                    _, sub, s = step
                    if sub == 0:
                        n = s - 2
                        if 0 <= n < len(NA_UNITS):
                            kind, hp, j = NA_UNITS[n]
                            dve.wait_ge(na_pv, n + 1)
                            if kind == "lat":
                                v = att[:, hp, 0:LAT].rearrange("p (r c) -> p r c", c=GRID)[:, :, j * QB:(j + 1) * QB]
                                nc.vector.tensor_copy(v, A[3][:, NKEY:512].rearrange("p (r c) -> p r c", r=ROWS)[:, :, ::-1]
                                                      ).then_inc(na_out, 1)
                            else:
                                nc.vector.tensor_copy(att[:, 2 * hp:2 * hp + 2, LAT:T],
                                                      A[3][:, 256:512].rearrange("p (i t) -> p i t", i=2)
                                                      ).then_inc(na_out, 1)
                        if s < len(NA_UNITS):
                            kind, hp, j = NA_UNITS[s]
                            b = s % 2
                            dve.wait_ge(na_sc, s + 1)
                            if s >= 2:
                                dve.wait_ge(na_tr, s - 1)
                            if kind == "lat":
                                if s == 0:
                                    dve.wait_ge(bias_zero, 1)
                                dve.wait_ge(bias_rd, 3 * hp + BTYPE[j] + 1)
                                nc.vector.tensor_tensor(sx[:, b], ps[:, 4:6, 0:NKEY], bm[:, BTYPE[j]],
                                                        ALU.add).then_inc(na_add, 1)
                                dve.wait_ge(na_add, s + 1)
                                nc.vector.tensor_reduce(small[:, 16:18], sx[:, b], X, ALU.max, negate=True).then_inc(na_max, 1)
                            else:
                                v = sx[:, b, :, 0:256]
                                nc.vector.tensor_copy(v, ps[:, 4:6, 0:256]).then_inc(na_add, 1)
                                dve.wait_ge(na_add, s + 1)
                                nc.vector.tensor_reduce(small[:, 16:20].rearrange("p (a i) -> p a i", a=2),
                                                        v.rearrange("p a (i k) -> p a i k", i=2), X, ALU.max,
                                                        negate=True).then_inc(na_max, 1)
                    if sub == 1 and s < len(NA_UNITS):
                        kind, hp, j = NA_UNITS[s]
                        b = s % 2
                        m = 2 if kind == "lat" else 4
                        dve.wait_ge(na_exp, s + 1)
                        link(nc.vector.reciprocal(small[:, 24:24 + m], small[:, 20:20 + m]))
                        for i in range(m):
                            v = sx[:, b, i, :] if m == 2 else sx[:, b, i // 2, (i % 2) * CTX:(i % 2 + 1) * CTX]
                            ins = nc.vector.tensor_scalar(v, v, small[:, 24 + i:25 + i], None, ALU.mult)
                        ins.then_inc(na_prob, 1)
                        dve.wait_ge(na_prob, s + 1)
                elif step[0] == "conv":
                    _, which, f = step
                    dve.wait_ge(dve_drain, drains("V", gid("cx", which, f, 1)))
                    if which:
                        dve.wait_ge(bo_lod, f + 1)
                    ft = 2 * which + f
                    w = [cols[:, R_CW + 4 * k + ft:R_CW + 4 * k + ft + 1] for k in range(3)]
                    u, y = cu[:, f, :], t1[:, f, :]
                    link(nc.vector.tensor_scalar(y, u, w[1], None, ALU.mult))
                    pieces = []
                    for lo, hi in ((0, LAT), (LAT, T)):
                        pieces += [(lo + 1, hi, -1, w[0]), (lo, hi - 1, 1, w[2])]
                    for j, (lo, hi, d, wk) in enumerate(pieces):
                        ins = nc.vector.scalar_tensor_tensor(y[:, lo:hi], u[:, lo + d:hi + d], wk, y[:, lo:hi],
                                                             ALU.mult, ALU.add)
                        if j < 3:
                            link(ins)
                    ins.then_inc(conv_rd, 1)
                elif step[0] == "mstat":
                    dve.wait_ge(dve_drain, drains("V", gid("mif", 0, 0, 1)))
                    nc.vector.scalar_tensor_tensor(st[0][:, :], lf[:, :], -1.0, lf[:, :], ALU.mult,
                                                   ALU.min).then_inc(f_neg, 1)
                    dve.wait_ge(f_ln, 1)
                    link(nc.vector.scalar_tensor_tensor(lf[:, :], lf[:, :], 0.0, st[2][:, :], ALU.min, ALU.subtract))
                    spans = ((0, LAT), (LAT, T))

                    def turned(dst, src):
                        nc.vector.tensor_copy(dst[0:32, :], src[0:32, :])
                        for lo, hi in spans:
                            ins = nc.vector.tensor_copy(dst[32:RW, lo:hi], src[32:RW, lo:hi][:, ::-1])
                        return ins

                    link(turned(st[0], ib))
                    link(turned(st[1], lf))
                    ones, zero, m0 = st[6], small[0:RW, 42:43], gbias[:, 2:3]
                    link(nc.vector.memset(ones[:, :], 1.0))
                    link(nc.vector.memset(zero, 0.0))
                    for c in range(TT):
                        ins = nc.vector.tensor_tensor_scan(st[2][:, tok(c)], ones[:, tok(c)], st[1][:, tok(c)], 0.0,
                                                           ALU.mult, ALU.add)
                    link(ins)
                    link(nc.vector.tensor_tensor(st[0][:, :], st[0][:, :], st[2][:, :], ALU.subtract))
                    mcur = m0
                    for c in range(TT):
                        if c == CH:
                            mcur = zero
                        end = (c + 1) * P
                        link(nc.vector.tensor_tensor_scan(st[3][:, tok(c)], st[0][:, tok(c)], st[0][:, tok(c)], mcur,
                                                          ALU.max, ALU.max))
                        nc.vector.tensor_scalar(st[4][:, tok(c)], st[3][:, tok(c)], -1.0, mcur, ALU.mult, ALU.add)
                        nc.vector.tensor_scalar(st[5][:, tok(c)], st[0][:, tok(c)], st[3][:, end - 1:end], None,
                                                ALU.subtract)
                        nxt = small[0:RW, 57 + c:58 + c] if c < CH else small[0:RW, 40:41]
                        ins = nc.vector.tensor_tensor(nxt, st[2][:, end - 1:end], st[3][:, end - 1:end], ALU.add)
                        if c == CH:
                            ins.then_inc(m_fin, 1)
                            dve.wait_ge(m_fin, 1)
                        else:
                            link(ins)
                        mcur = nxt
                    nc.vector.scalar_tensor_tensor(st[2][:, :], st[2][:, :], -1.0, st[3][:, :], ALU.mult,
                                                   ALU.subtract).then_inc(s_exp_in, 1)
                    dve.wait_ge(s_exp_in, 1)
                    dve.wait_ge(stored, 32)
                    turned(ib, st[0])
                    link(turned(mnat, st[3]))
                    dve.wait_ge(s_exp, 1)
                    turned(lf, st[4])
                    turned(st[1], st[5])
                    turned(st[6], st[2]).then_inc(nat_rd, 1)
                elif step[0] == "mcols":
                    for i, c0, c1 in ((0, 0, 3), (1, 3, TT)):
                        dve.wait_ge(ms_tr, c1)
                        src = A[i][:, 0:(c1 - c0) * 4 * RW].rearrange("p (c q r) -> p c q r", q=4, r=RW)
                        nc.vector.tensor_copy(mcols[:, c0:c1, :, 0:4], src[:, :, :, 0:4])
                        nc.vector.tensor_copy(mcols[:, c0:c1, :, 4:8], src[:, :, :, 32:36]).then_inc(ms_rd, 1)
                    dve.wait_ge(ms_tr, TT + 1)
                    nc.vector.tensor_copy(dec[:, :, :], A[2][:, 0:32].rearrange("p (r c) -> p r c", r=8)).then_inc(ms_rd, 1)
                    dve.wait_ge(ms_rd, 3)
                    dve.wait_ge(state_in, 32)
                elif step[0] == "ml":
                    _, sub, n = step
                    ch, dr, hp, first, last = ML_UNITS[n]
                    b = n % 2
                    if sub == 0:
                        dve.wait_ge(ml_a, n + 1)
                        for i in range(2):
                            r = dr * 4 + 2 * hp + i
                            ins = nc.vector.scalar_tensor_tensor(e_sb[:, b, i, :], A[0][:, i * P:(i + 1) * P],
                                                                 mcols[:, ch, 0, r:r + 1], mask_m[:, dr, :],
                                                                 ALU.subtract, ALU.max)
                        ins.then_inc(ml_dm, 1)
                        dve.wait_ge(ml_e, n + 1)
                        nc.vector.tensor_tensor(st_sb[:, b], A[1][:, 0:256].rearrange("p (i t) -> p i t", i=2),
                                                e_sb[:, b], ALU.mult).then_inc(ml_st, 1)
                    else:
                        dve.wait_ge(ml_b, n + 1)
                        intra = A[3][:, 0:258].rearrange("p (i e) -> p i e", i=2)
                        upd = A[1][:, 0:258].rearrange("p (i e) -> p i e", i=2)
                        if ch < CH:
                            dve.wait_ge(ml_tmp, n - 3)
                            ins = nc.vector.tensor_tensor(num_sb[:, :, :], intra, tmp_sb[:, :, :], ALU.add)
                            if not last:
                                link(ins)
                                for i in range(2):
                                    r = dr * 4 + 2 * hp + i
                                    ins = nc.vector.scalar_tensor_tensor(cl[:, r, :], cl[:, r, :], dec[:, r, ch:ch + 1],
                                                                         upd[:, i, :], ALU.mult, ALU.add)
                        else:
                            link(nc.vector.tensor_copy(num_sb[:, :, :], intra))
                            if n >= 2:
                                dve.wait_ge(c_out[n % 2], 32)
                            ins = nc.vector.tensor_copy(cout[:, n % 2], upd)
                        ins.then_inc(ml_c, 1)
                        dve.wait_ge(ml_c, n + 1)
                        den = num_sb[:, :, 128]
                        d = small[:, 24:26]
                        r0 = dr * 4 + 2 * hp
                        link(nc.vector.scalar_tensor_tensor(d, den, -1.0, den, ALU.mult, ALU.max))
                        link(nc.vector.tensor_tensor(d, d, mcols[:, ch, 3, r0:r0 + 2], ALU.max))
                        link(nc.vector.reciprocal(d, d))
                        for i in range(2):
                            hd = 2 * hp + i
                            v = hsum[:, ch, hd * 128:(hd + 1) * 128]
                            if (ch, hd) in written:
                                ins = nc.vector.scalar_tensor_tensor(v, num_sb[:, i, 0:128], d[:, i:i + 1], v,
                                                                     ALU.mult, ALU.add)
                            else:
                                ins = nc.vector.tensor_scalar(v, num_sb[:, i, 0:128], d[:, i:i + 1], None, ALU.mult)
                            written.add((ch, hd))
                        ins.then_inc(ml_h, 1)
                        dve.wait_ge(ml_h, n + 1)
                elif step[0] == "hm":
                    _, sub, c = step
                    v = small[:, 16 + 4 * c:20 + 4 * c] if c < 4 else small[:, 32:36]
                    if sub == 0:
                        sq = st_sb[:, :, :, :].rearrange("p a b c -> p (a b c)")
                        link(nc.vector.tensor_tensor(sq, hsum[:, c, :], hsum[:, c, :], ALU.mult))
                        nc.vector.tensor_reduce(v, sq.rearrange("p (h d) -> p h d", h=MH), X, ALU.add).then_inc(hm_sq, 1)
                        dve.wait_ge(hm_sq, c + 1)
                    elif sub == 1:
                        dve.wait_ge(hm_rstd, c + 1)
                        y = hsum[:, c, :].rearrange("p (h d) -> p h d", h=MH)
                        nc.vector.tensor_tensor(y, y, v.unsqueeze(2).to_broadcast([P, MH, 128]), ALU.mult).then_inc(hm_nrm, 1)
                    else:
                        dve.wait_ge(hm_tr, c + 1)
                        dve.wait_ge(mo_rd, 8)
                        for hd in range(MH):
                            ins = nc.vector.scalar_tensor_tensor(
                                hmt[:, hd, tok(c)], A[c % 4][:, hd * P:(hd + 1) * P],
                                cols[:, R_MG + hd:R_MG + hd + 1], mo[:, hd, tok(c)], ALU.mult, ALU.mult)
                        ins.then_inc(hm_out, 1)
                elif step[0] == "out_split":
                    for k in range(step[1], step[2]):
                        dve.wait_ge(mg_hid, k + 1)
                        nc.vector.scalar_tensor_tensor(h_lo[:, k, :], merged[:, k, :], 0.5,
                                                       h_hi[:, k, :].bitcast(F32), ALU.mult,
                                                       ALU.subtract).then_inc(mg_lod, 1)
                elif step[0] == "down_start":
                    t = step[1]
                    dve.wait_ge(ffs_hi, t + 1)
                    n = DOWN_TILES[0]
                    nc.vector.tensor_tensor(h_lo[:, 0:n, tok(t)], ff[:, 0:n, tok(t)],
                                            h_hi[:, 0:n, tok(t)].bitcast(F32), ALU.subtract).then_inc(ffs_lo, 1)
                elif step[0] == "resid":
                    t = step[1]
                    dve.wait_ge(y_rstd, t + 1)
                    dve.wait_ge(dve_drain, drains("V", gid("out", (1, 1, ROUND[t]), 1, t)))
                    dve.wait_ge(xb_in[t % 2], 16 * (t // 2 + 1))
                    nc.vector.scalar_tensor_tensor(x1[:, t, :], x1[:, t, :], small[:, t:t + 1], xb[:, t % 2, :],
                                                   ALU.mult, ALU.add).then_inc(x1_rd, 1)
                elif step[0] == "turn2":
                    t = step[1]
                    cnd = 0 if t < CH else 1
                    for hh in range(2):
                        dve.wait_ge(n2_tr, 2 * t + hh + 1)
                        if t >= 2:
                            dve.wait_ge(n2_lod, t - 1)
                        b = 2 + hh
                        for kk in range(4):
                            k = 4 * hh + kk
                            ins = nc.vector.tensor_scalar(h32[:, t % 2, k, :], ps[:, b, kk * P:(kk + 1) * P],
                                                          mod[:, 2, k, cnd:cnd + 1], mod[:, 3, k, cnd:cnd + 1],
                                                          ALU.mult, ALU.add)
                        ins.then_inc(n2_ev, 1)
                elif step[0] == "split2":
                    t = step[1]
                    dve.wait_ge(n2_hid, t + 1)
                    nc.vector.tensor_tensor(h_lo[:, :, tok(t)], h32[:, t % 2], h_hi[:, :, tok(t)].bitcast(F32),
                                            ALU.subtract).then_inc(n2_lod, 1)
                elif step[0] == "final":
                    t = step[1]
                    dve.wait_ge(z_rstd, t + 1)
                    dve.wait_ge(dve_drain, drains("V", gid("down", (1, 5), 1, t)))
                    r = small[:, 16 + t:17 + t]
                    nc.vector.scalar_tensor_tensor(x1[:, t, 0:512], y2[:, t, :], r, x1[:, t, 0:512], ALU.mult, ALU.add)
                    nc.vector.scalar_tensor_tensor(x1[:, t, 512:D], yb[:, t % 2, :], r, x1[:, t, 512:D],
                                                   ALU.mult, ALU.add).then_inc(fin_rd, 1)
                    dve.wait_ge(fin_rd, t + 1)

        @block.tensor
        def _(pe):
            def bank_free(g, rnd=0):
                prev = last_user(GROUPS[g]["bank"], g)
                if prev is not None:
                    e = GROUPS[prev]["eng"]
                    pe.wait_ge(act_drain if e == "A" else dve_drain, drains(e, prev) + DRAINS_A_ROUND * rnd)

            def three(dst, wh, wl, xh, xl, first, last):
                nc.tensor.matmul(dst, wh, xh, start=first, stop=False)
                nc.tensor.matmul(dst, wh, xl, start=False, stop=False)
                return nc.tensor.matmul(dst, wl, xh, start=False, stop=last)

            def block_ready(b, rnd=0):
                pe.wait_ge(hi_done, b + 1 + BLOCKS_HELD * rnd)
                wait_lo(pe, b, rnd)

            def group(g, rnd=0):
                x = GROUPS[g]
                kind, n, what = x["kind"], x["unit"], x["what"]
                which = UNITS[n][1]
                full = ps[:, x["bank"], :]
                if kind not in ("out", "down"):
                    bank_free(g, rnd)
                if kind == "ada_row":
                    for k in range(KD):
                        nc.tensor.matmul(full[0:4, 0:UW], cond[:, k, :], weight(w_hi, n, k), start=(k == 0), stop=False)
                        ins = nc.tensor.matmul(full[0:4, 0:UW], cond[:, k, :], weight(w_lo, n, k), start=False,
                                               stop=(k == KD - 1))
                elif kind == "ada_col":
                    m = which[0]
                    rowg = next(i for i in range(g - 1, -1, -1) if GROUPS[i]["kind"] == "ada_row" and GROUPS[i]["unit"] == n)
                    pe.wait_ge(act_drain, drains("A", rowg))
                    ar = adarow[:, ada_slot(n), :]
                    if m in (2, 5):
                        for c in range(2):
                            ins = nc.tensor.matmul(full[:, c * UW:(c + 1) * UW], sel[:, c, :], ar, start=True, stop=True)
                    else:
                        for k in range(2):
                            ins = nc.tensor.matmul(full[:, 2 * k:2 * k + 2], ar[:, k * P:(k + 1) * P], sel[:, :, 0],
                                                   start=True, stop=True)
                elif kind == "vt":
                    f, c = what
                    pe.wait_ge(act_drain, drains("A", gid("v", which, f, 1)))
                    for i in range(4 if c < 2 else 1):
                        ins = nc.tensor.transpose(full[:, i * P:(i + 1) * P], vg[:, 4 * c + i, :], ident)
                elif kind == "mvt":
                    f, c = what
                    pe.wait_ge(act_drain, drains("A", gid("mv", which, f, 1)))
                    for i in range(4 if c == 0 else 1):
                        ins = nc.tensor.transpose(full[:, i * P:(i + 1) * P], vg[:, 4 * c + i, :], ident)
                elif kind == "kout":
                    for i in range(4):
                        ins = nc.tensor.transpose(full[:, i * P:(i + 1) * P], nak[:, i, LAT:T], ident)
                elif kind in ("out", "down"):
                    part(kind, what[0], what[1], 1 if kind == "out" else 5).then_inc(gemm_done, 1)
                    return
                else:
                    f, h = what
                    if kind in ("fg", "fu") and which == 0:
                        pe.wait_ge(n2_lod, 3 if h == 0 else TT)
                    for k in range(UNITS[n][2]):
                        if kind == "br":
                            xh, xl = bo_hi, bo_lo
                            pe.wait_ge(bo_lod, 4 * (2, 0, 1).index(which[0]) + k + 1)
                        else:
                            xh, xl = h_hi, h_lo
                            if n == 8:
                                pe.wait_ge(h_lod, k + 1)
                        ins = three(full[:, 0:HT], weight(w_hi, n, k, f), weight(w_lo, n, k, f), xh[:, k, half(h)], xl[:, k, half(h)],
                                    k == 0, k == UNITS[n][2] - 1)
                ins.then_inc(gemm_done, 1)

            def part(kind, c, t, i):
                n = UNIT_OF[(kind, (c, i, ROUND[t]) if kind == "out" else (c, i))]
                g = gid(kind, (c, 1, ROUND[t]) if kind == "out" else (c, 5), c, t)
                if i == 0:
                    bank_free(g)
                kc = UNITS[n][2]
                dst = ps[:, GROUPS[g]["bank"], :]
                lastu = i == (1 if kind == "out" else 5)
                for k in range(kc):
                    if kind == "out":
                        kk = 4 * i + k
                        if c == 0 and t == 0:
                            pe.wait_ge(mg_lod, kk + 1)
                    else:
                        o = 6 * c + i
                        if k == 0 and o == 0:
                            pe.wait_ge(ffs_lo, t + 1)
                        elif k == 0 and t == 0:
                            pe.wait_ge(ffs_lo, TT + 2 * o)
                        kk = 4 * (o % 2) + k
                    ins = three(dst, h_hi[:, kk, tok(t)], h_lo[:, kk, tok(t)], weight(w_hi, n, k), weight(w_lo, n, k),
                                i == 0 and k == 0, lastu and k == kc - 1)
                return ins

            pe.wait_ge(const_in, 16)
            pe.wait_ge(rows_in, 16)
            nc.tensor.transpose(A[0][:, 0:NROWS], rows[:, :], ident[0:NROWS, 0:NROWS]).then_inc(cols_tr, 1)
            pe.wait_ge(cond_rd, 1)
            for step in PROGRAM:
                if step[0] == "ff_loop":
                    with pe.Fori(0, FF_ROUNDS) as rnd:
                        for s in FF_BODY:
                            if s[0] == "use":
                                block_ready(s[1], rnd)
                            elif s[0] == "group":
                                group(s[1], rnd)
                elif step[0] == "xturn":
                    k = step[1]
                    if k == 0:
                        pe.wait_ge(x_nrm, TT)
                    if k >= 2:
                        pe.wait_ge(xt_act if k % 2 else xt_dve, k // 2)
                    for t in range(CH):
                        ins = nc.tensor.transpose(A[k % 2][:, t * P:(t + 1) * P], xt[:, t, tok(k)], ident)
                    ins.then_inc(xl_tr, 1)
                    ins = nc.tensor.transpose(A[2 + k // 4][:, (k % 4) * P:(k % 4 + 1) * P], xt[:, CH, tok(k)], ident)
                    if k % 4 == 3:
                        ins.then_inc(xc_tr, 1)
                elif step[0] == "kc":
                    pe.wait_ge(kc_in, 16)
                    pe.wait_ge(xt_act, 4)
                    for i in range(4):
                        ins = nc.tensor.transpose(A[1][:, i * P:(i + 1) * P], kcr[:, i * P:(i + 1) * P], ident)
                    ins.then_inc(kc_tr, 1)
                elif step[0] == "use":
                    block_ready(step[1])
                elif step[0] == "group":
                    group(step[1])
                elif step[0] == "part":
                    part(*step[1:]).then_inc(part_done, 1)
                elif step[0] == "na":
                    _, sub, s = step
                    if sub == 0:
                        n = s - 2
                        if 0 <= n < len(NA_UNITS):
                            kind, hp, j = NA_UNITS[n]
                            pe.wait_ge(na_pt, n + 1)
                            if n == 0:
                                pe.wait_ge(vc_in, 16)
                            last_v = gid("vt", 0 if (hp < 2 if kind == "lat" else hp == 0) else 1, 1, 2)
                            pe.wait_ge(dve_drain, drains("V", last_v))
                            for i in range(2):
                                dst = A[3][64 * i:64 * i + 64, :]
                                if kind == "lat":
                                    hc = slice((2 * hp + i) * DH, (2 * hp + i + 1) * DH)
                                    for c in range(3):
                                        src = vtok[:, 2 * j + c, hc] if c < 2 else vtok[:, 9, hc]
                                        ins = nc.tensor.matmul(dst[:, NKEY:512], src, pt[:, n % 2, i, c * P:(c + 1) * P],
                                                               start=(c == 0), stop=(c == 2))
                                else:
                                    for q in range(2):
                                        hd = 2 * (2 * hp + q) + i
                                        ins = nc.tensor.matmul(dst[:, 256 + q * P:256 + (q + 1) * P],
                                                               vtok[:, 8, hd * DH:(hd + 1) * DH],
                                                               pt[:, n % 2, i, q * P:(q + 1) * P], start=True, stop=True)
                            ins.then_inc(na_pv, 1)
                        if s < len(NA_UNITS):
                            kind, hp, j = NA_UNITS[s]
                            p = (hp if kind == "lat" else 2 * hp) // 2
                            pe.wait_ge(act_drain, drains("A", gid("k", p, 1, 1)))
                            if s:
                                pe.wait_ge(na_add, s)
                            else:
                                pe.wait_ge(kc_rd, 1)
                            for i in range(2):
                                pp = slice(64 * i, 64 * i + 64)
                                if kind == "lat":
                                    q = naq[pp, hp, j * P:(j + 1) * P]
                                    kk = nak[pp, hp, 0:LAT].rearrange("p (r c) -> p r c", c=GRID)[
                                        :, :, KSTART[j]:KSTART[j] + KB]
                                    nc.tensor.matmul(A[i][:, 0:256], q, kk, start=True, stop=True)
                                    ins = nc.tensor.matmul(A[i][:, 256:NKEY], q, kct[pp, hp, :], start=True, stop=True)
                                else:
                                    for c in range(2):
                                        ins = nc.tensor.matmul(A[i][:, c * P:(c + 1) * P], naq[pp, 2 * hp + c, LAT:T],
                                                               nak[pp, 2 * hp + c, LAT:T], start=True, stop=True)
                            ins.then_inc(na_sc, 1)
                    if sub == 1 and 0 <= s - 1 < len(NA_UNITS):
                        n = s - 1
                        kind = NA_UNITS[n][0]
                        pe.wait_ge(na_prob, n + 1)
                        if n:
                            pe.wait_ge(na_out, n)
                            pe.wait_ge(na_pt, n)
                        else:
                            pe.wait_ge(xc_dve, 2)
                        for i in range(2):
                            for c in range(3 if kind == "lat" else 2):
                                ins = nc.tensor.transpose(A[2 + i][:, c * P:(c + 1) * P],
                                                          sx[:, n % 2, i, c * P:(c + 1) * P], ident)
                        ins.then_inc(na_tr, 1)
                elif step[0] == "mcols":
                    pe.wait_ge(nat_rd, 1)
                    for c in range(TT):
                        for q, src in enumerate((ib, lf, st[1], st[6])):
                            col = (4 * (c % 3) + q) * RW
                            ins = nc.tensor.transpose(A[c // 3][:, col:col + RW], src[:, tok(c)],
                                                      ident[0:RW, 0:RW])
                        ins.then_inc(ms_tr, 1)
                    for dr in range(2):
                        for hd in range(MH):
                            r = dr * 4 + hd
                            sr = dr * 32 + hd
                            e0 = P - 1 if dr == 0 else 0
                            ins = nc.tensor.matmul(A[2][:, r * CH:(r + 1) * CH],
                                                   ident[0:RW, sr:sr + 1].to_broadcast([RW, P]),
                                                   lf[:, e0:e0 + (CH - 1) * P + 1:P], start=True, stop=True)
                    ins.then_inc(ms_tr, 1)
                elif step[0] == "ml":
                    _, sub, n = step
                    ch, dr, hp, first, last = ML_UNITS[n]
                    b = n % 2
                    if sub == 0:
                        pe.wait_ge(ms_rd, 3)
                        if n:
                            pe.wait_ge(ml_c, n)
                        for i in range(2):
                            hd = 2 * hp + i
                            sr = dr * 32 + hd
                            pr = slice(i * P, (i + 1) * P)
                            nc.tensor.matmul(A[0][:, pr], ident[0:RW, sr:sr + 1].to_broadcast([RW, P]),
                                             mnat[:, tok(ch)], start=True, stop=True)
                            nc.tensor.matmul(A[1][:, pr], mk[:, hd, tok(ch)], mq[:, hd, tok(ch)], start=True, stop=True)
                            ins = nc.tensor.transpose(A[2][:, pr], mk[:, hd, tok(ch)], ident)
                        ins.then_inc(ml_a, 1)
                    else:
                        pe.wait_ge(ml_st, n + 1)
                        pe.wait_ge(ml_kw, n + 1)
                        if n == 0:
                            pe.wait_ge(mv_ones, 1)
                            pe.wait_ge(dve_drain, drains("V", gid("mvt", 1, 1, 1)))
                        for i in range(2):
                            hd = 2 * hp + i
                            r = dr * 4 + hd
                            pr = slice(i * 129, (i + 1) * 129)
                            ins = nc.tensor.matmul(A[3][:, pr], st_sb[:, b, i, :], mv[:, ch, hd, :], start=True, stop=True)
                            if ch < CH:
                                ins = nc.tensor.matmul(A[0][:, pr], mq[:, hd, tok(ch)], cl[:, r, :], start=True, stop=True)
                            if ch == CH or not last:
                                ins = nc.tensor.matmul(A[1][:, pr], kw_sb[:, b, i, :], mv[:, ch, hd, :], start=True, stop=True)
                        ins.then_inc(ml_b, 1)
                elif step[0] == "hm" and step[1] == 2:
                    c = step[2]
                    pe.wait_ge(hm_nrm, c + 1)
                    if c >= 4:
                        pe.wait_ge(hm_out, c - 3)
                    for hd in range(MH):
                        ins = nc.tensor.transpose(A[c % 4][:, hd * P:(hd + 1) * P], hsum[:, c, hd * 128:(hd + 1) * 128],
                                                  ident)
                    ins.then_inc(hm_tr, 1)
                elif step[0] == "out_start":
                    pe.wait_ge(hm_out, TT)
                elif step[0] == "turn2":
                    t = step[1]
                    pe.wait_ge(xn_rd, t + 1)
                    for hh in range(2):
                        m = 2 * t + hh
                        if m >= 2:
                            pe.wait_ge(n2_ev, m - 1)
                        for kk in range(4):
                            ins = nc.tensor.transpose(ps[:, 2 + hh, kk * P:(kk + 1) * P],
                                                      xn[:, t % 2, tok(4 * hh + kk)], ident)
                        ins.then_inc(n2_tr, 1)


def constants():
    import numpy as np
    c = np.zeros((P, 736), np.float32)
    c[:, 0:128] = np.eye(P)
    s, t = np.arange(P)[:, None], np.arange(P)[None, :]
    c[:, 128:256] = np.where(s > t, BIG, 0)
    c[:, 256:384] = np.where(s < t, BIG, 0)
    for y, j in enumerate((0, 1, 3)):
        q = j * QB + QB - 1 - np.arange(P)[:, None] % QB
        k = KSTART[j] + np.arange(KB)[None, :]
        lo = np.clip(q - KW // 2, 0, GRID - KW)
        c[:, 384 + y * KB:384 + (y + 1) * KB] = np.where((k >= lo) & (k < lo + KW), 0, -BIG)
    for v in range(2):
        c[v, 480 + v * P:480 + (v + 1) * P] = 1
        c[v + 2, 480 + v * P:480 + (v + 1) * P] = 1
    return c


_WEIGHTS = ["w_ada", "w_in", "w_br_na", "w_br_m", "w_br_cv", "w_out", "w_ffn_gate", "w_ffn_up", "w_ffn_down"]
_PLAIN = ["x_prompt", "x_sample", "cache_k", "cache_v", "state_C", "state_n", "b_ada", "g_post_mix", "g_post_ffn"]
_OUTS = dict(yp=(1, CTX, D), ys=(1, LAT, D), k=(1, 1, HEADS, CTX, DH), v=(1, 1, HEADS, CTX, DH),
             C=(1, 1, 2, MH, DK, 128), n=(1, 1, 2, MH, DK), m=(1, 1, 2, MH))


def kernel(**inputs):
    import numpy as np
    import concourse.bacc as bacc
    from concourse.bass_utils import run_bass_kernel_spmd

    x = {n: np.ascontiguousarray(v) for n, v in inputs.items()}
    given = {n: x[n] for n in _WEIGHTS + _PLAIN}
    given["consts"] = constants()
    given["rows"] = np.concatenate([x[n].reshape(-1, P) for n in (
        "b_ada", "g_pre_mix", "g_pre_ffn", "b_gate", "m_norm_g", "conv_w", "c", "c_ctx")])
    rpb = np.zeros((HEADS, 16, 64), x["na_rpb"].dtype)
    rpb[:, 0:15, 16:47] = x["na_rpb"][0]
    given["rpb"] = rpb
    gb = np.zeros((RW, 3), x["m_b_i"].dtype)
    for d in range(2):
        gb[32 * d:32 * d + MH, 0] = x["m_b_i"][0, d]
        gb[32 * d:32 * d + MH, 1] = x["m_b_f"][0, d]
        gb[32 * d:32 * d + MH, 2] = x["state_m"][0, 0, d]
    given["gbias"] = gb

    nc = bacc.Bacc("TRN2", target_bir_lowering=False, num_devices=1)
    a = {n: nc.dram_tensor("in_" + n, v.shape, F32, kind="ExternalInput").ap() for n, v in given.items()}
    out = {n: nc.dram_tensor("out_" + n, shape, F32, kind="ExternalOutput").ap() for n, shape in _OUTS.items()}
    program(nc, a, out)
    r = run_bass_kernel_spmd(nc, [{"in_" + n: v for n, v in given.items()}], core_ids=[0])
    return tuple(r.results[0]["out_" + n] for n in _OUTS)
```
